# Optimizing a Trainium2 kernel written in Bass

```python
import jax, jax.numpy as jnp
from jax import lax
import numpy as np

D_MODEL = 1024
BATCH = 1
SEQ = 512
DEPTH = 2

GRID_W = 64
CTX_LEN = 256
N_Q_HEADS = 8
N_KV_HEADS = 2
GROUP = N_Q_HEADS // N_KV_HEADS
HEAD_DIM = 64
ATTN_WIDTH = N_Q_HEADS * HEAD_DIM
KV_WIDTH = N_KV_HEADS * HEAD_DIM
CONV_WIDTH = D_MODEL - ATTN_WIDTH
IN_WIDTH = ATTN_WIDTH + 2 * KV_WIDTH + 2 * CONV_WIDTH
CONV_KERNEL = 31
CONV_PAD = CONV_KERNEL // 2
WINDOW = 128
BLOCK_Q = 128
SPAN = BLOCK_Q + 2 * WINDOW
D_FF = -(-8 * D_MODEL // (3 * 256)) * 256
ROPE_BASE = 10000.0
ROPE_HALF = HEAD_DIM // 2
ROPE_FREQS = HEAD_DIM // 4
EPS = 1e-6
NEG_INF = -1e30
SCALE = HEAD_DIM ** -0.5

kernel_name = "hybrid_swa_conformer_dit"

def rmsnorm(x, g):
    xf = x.astype(jnp.float32)
    y = xf * lax.rsqrt(jnp.mean(xf * xf, axis=-1, keepdims=True) + EPS)
    return (y * g.astype(jnp.float32)).astype(x.dtype)

def layernorm(x, g, b):
    xf = x.astype(jnp.float32)
    mu = jnp.mean(xf, axis=-1, keepdims=True)
    var = jnp.mean(jnp.square(xf - mu), axis=-1, keepdims=True)
    y = (xf - mu) * lax.rsqrt(var + EPS)
    return (y * g.astype(jnp.float32) + b.astype(jnp.float32)).astype(x.dtype)

def modulate(h, shift, scale):
    return h * (1 + scale) + shift

def axial_angles(n_tokens):
    rows = n_tokens // GRID_W
    r = jnp.broadcast_to(jnp.arange(rows, dtype=jnp.float32)[:, None], (rows, GRID_W)).reshape(-1)
    col = jnp.broadcast_to(jnp.arange(GRID_W, dtype=jnp.float32)[None, :], (rows, GRID_W)).reshape(-1)
    freqs = ROPE_BASE ** (-jnp.arange(ROPE_FREQS, dtype=jnp.float32) / ROPE_FREQS)
    return r[:, None] * freqs, col[:, None] * freqs

def rope_1d(x, ang):
    cos = jnp.cos(ang)[:, None, :].astype(x.dtype)
    sin = jnp.sin(ang)[:, None, :].astype(x.dtype)
    x1, x2 = x[..., :ROPE_FREQS], x[..., ROPE_FREQS:]
    return jnp.concatenate([x1 * cos - x2 * sin, x1 * sin + x2 * cos], axis=-1)

def rope_2d(x, ang_r, ang_c):
    return jnp.concatenate([rope_1d(x[..., :ROPE_HALF], ang_r), rope_1d(x[..., ROPE_HALF:], ang_c)], axis=-1)

def split_in(p):
    q = p[..., :ATTN_WIDTH]
    k = p[..., ATTN_WIDTH:ATTN_WIDTH + KV_WIDTH]
    v = p[..., ATTN_WIDTH + KV_WIDTH:ATTN_WIDTH + 2 * KV_WIDTH]
    u = p[..., ATTN_WIDTH + 2 * KV_WIDTH:]
    return q, k, v, u

def latent_attention(q, k, v, k_ctx, v_ctx, sink):
    B, N = q.shape[0], q.shape[1]
    L = k_ctx.shape[1]
    nb = N // BLOCK_Q
    qb = q.reshape(B, nb, BLOCK_Q, N_KV_HEADS, GROUP, HEAD_DIM)
    pad = ((0, 0), (WINDOW, WINDOW), (0, 0), (0, 0))
    kp = jnp.pad(k, pad)
    vp = jnp.pad(v, pad)
    idx = jnp.arange(nb)[:, None] * BLOCK_Q + jnp.arange(SPAN)[None, :]
    kb = kp[:, idx]
    vb = vp[:, idx]
    qpos = jnp.arange(nb)[:, None] * BLOCK_Q + jnp.arange(BLOCK_Q)[None, :]
    kpos = idx - WINDOW
    valid = ((jnp.abs(qpos[:, :, None] - kpos[:, None, :]) <= WINDOW)
             & (kpos[:, None, :] >= 0) & (kpos[:, None, :] < N))
    s_loc = jnp.einsum('bnqhgd,bnkhd->bnhgqk', qb, kb).astype(jnp.float32) * SCALE
    s_loc = jnp.where(valid[None, :, None, None], s_loc, NEG_INF)
    s_ctx = jnp.einsum('bnqhgd,bchd->bnhgqc', qb, k_ctx).astype(jnp.float32) * SCALE
    s_sink = jnp.broadcast_to(sink.astype(jnp.float32).reshape(N_KV_HEADS, GROUP, 1, 1),
                              (B, nb, N_KV_HEADS, GROUP, BLOCK_Q, 1))
    p = jax.nn.softmax(jnp.concatenate([s_loc, s_ctx, s_sink], axis=-1), axis=-1).astype(v.dtype)
    o = (jnp.einsum('bnhgqk,bnkhd->bnqhgd', p[..., :SPAN], vb)
         + jnp.einsum('bnhgqc,bchd->bnqhgd', p[..., SPAN:SPAN + L], v_ctx))
    return o.reshape(B, N, ATTN_WIDTH)

def context_attention(q_c, k_c, v_c, sink):
    B, L = q_c.shape[0], q_c.shape[1]
    qg = q_c.reshape(B, L, N_KV_HEADS, GROUP, HEAD_DIM)
    s = jnp.einsum('bqhgd,bkhd->bhgqk', qg, k_c).astype(jnp.float32) * SCALE
    s_sink = jnp.broadcast_to(sink.astype(jnp.float32).reshape(N_KV_HEADS, GROUP, 1, 1),
                              (B, N_KV_HEADS, GROUP, L, 1))
    p = jax.nn.softmax(jnp.concatenate([s, s_sink], axis=-1), axis=-1)[..., :L].astype(v_c.dtype)
    o = jnp.einsum('bhgqk,bkhd->bqhgd', p, v_c)
    return o.reshape(B, L, ATTN_WIDTH)

def conv_module(u, w_dw, b_dw, ln_g, ln_b):
    z = u[..., :CONV_WIDTH] * jax.nn.sigmoid(u[..., CONV_WIDTH:])
    z = lax.conv_general_dilated(z, w_dw[:, None, :], window_strides=(1,),
                                 padding=((CONV_PAD, CONV_PAD),),
                                 dimension_numbers=('NWC', 'WIO', 'NWC'),
                                 feature_group_count=CONV_WIDTH) + b_dw
    return jax.nn.silu(layernorm(z, ln_g, ln_b))

def merge_groups(a_out, cv_out, g_a, g_c, w_o):
    return jnp.concatenate([rmsnorm(a_out, g_a), rmsnorm(cv_out, g_c)], axis=-1) @ w_o

def swiglu(h, w_gu, w_dn):
    gu = h @ w_gu
    return (jax.nn.silu(gu[..., :D_FF]) * gu[..., D_FF:]) @ w_dn

def setup_inputs(seed: int = 0) -> dict:
    key = jax.random.key(seed)
    ks = jax.random.split(key, 20)
    f32 = jnp.float32
    nrm = lambda k, shape, s: jax.random.normal(k, shape, f32) * s
    return {
        "x": nrm(ks[0], (BATCH, SEQ, D_MODEL), 1.0),
        "c": nrm(ks[1], (BATCH, D_MODEL), 1.0),
        "ctx": nrm(ks[2], (BATCH, CTX_LEN, D_MODEL), 1.0),
        "c_ctx": nrm(ks[3], (D_MODEL,), 1.0),
        "w_ada": nrm(ks[4], (DEPTH, D_MODEL, 6 * D_MODEL), D_MODEL ** -0.5),
        "b_ada": nrm(ks[5], (DEPTH, 6 * D_MODEL), 0.02),
        "g_mix": 1.0 + nrm(ks[6], (DEPTH, D_MODEL), 0.05),
        "w_in": nrm(ks[7], (DEPTH, D_MODEL, IN_WIDTH), D_MODEL ** -0.5),
        "attn_sink": nrm(ks[8], (DEPTH, N_Q_HEADS), 1.0),
        "w_dw": nrm(ks[9], (DEPTH, CONV_KERNEL, CONV_WIDTH), CONV_KERNEL ** -0.5),
        "b_dw": nrm(ks[10], (DEPTH, CONV_WIDTH), 0.02),
        "ln_g": 1.0 + nrm(ks[11], (DEPTH, CONV_WIDTH), 0.05),
        "ln_b": nrm(ks[12], (DEPTH, CONV_WIDTH), 0.02),
        "g_attn_out": 1.0 + nrm(ks[13], (DEPTH, ATTN_WIDTH), 0.05),
        "g_conv_out": 1.0 + nrm(ks[14], (DEPTH, CONV_WIDTH), 0.05),
        "w_out": nrm(ks[15], (DEPTH, D_MODEL, D_MODEL), D_MODEL ** -0.5),
        "g_ffn": 1.0 + nrm(ks[16], (DEPTH, D_MODEL), 0.05),
        "w_gate_up": nrm(ks[17], (DEPTH, D_MODEL, 2 * D_FF), D_MODEL ** -0.5),
        "w_down": nrm(ks[18], (DEPTH, D_FF, D_MODEL), D_FF ** -0.5),
        "g_final": 1.0 + nrm(ks[19], (D_MODEL,), 0.05),
    }

def reference(x, c, ctx, c_ctx, w_ada, b_ada, g_mix, w_in, attn_sink, w_dw, b_dw, ln_g, ln_b,
              g_attn_out, g_conv_out, w_out, g_ffn, w_gate_up, w_down, g_final):
    B, N = x.shape[0], x.shape[1]
    L = ctx.shape[1]
    ang_r, ang_c = axial_angles(N)
    silu_c = jax.nn.silu(c)
    silu_cc = jax.nn.silu(c_ctx)
    for l in range(DEPTH):
        last = l == DEPTH - 1
        mod = (silu_c @ w_ada[l] + b_ada[l])[:, None, :]
        sh1, sc1, gt1, sh2, sc2, gt2 = jnp.split(mod, 6, axis=-1)
        mod_c = silu_cc @ w_ada[l] + b_ada[l]
        csh1, csc1, cgt1, csh2, csc2, cgt2 = jnp.split(mod_c, 6, axis=-1)

        h = modulate(rmsnorm(x, g_mix[l]), sh1, sc1)
        hc = modulate(rmsnorm(ctx, g_mix[l]), csh1, csc1)
        q, k, v, u = split_in(h @ w_in[l])
        q = rope_2d(q.reshape(B, N, N_Q_HEADS, HEAD_DIM), ang_r, ang_c)
        k = rope_2d(k.reshape(B, N, N_KV_HEADS, HEAD_DIM), ang_r, ang_c)
        v = v.reshape(B, N, N_KV_HEADS, HEAD_DIM)
        if last:
            kv_c = hc @ w_in[l][:, ATTN_WIDTH:ATTN_WIDTH + 2 * KV_WIDTH]
            k_c, v_c = kv_c[..., :KV_WIDTH], kv_c[..., KV_WIDTH:]
        else:
            q_c, k_c, v_c, u_c = split_in(hc @ w_in[l])
        k_c = k_c.reshape(B, L, N_KV_HEADS, HEAD_DIM)
        v_c = v_c.reshape(B, L, N_KV_HEADS, HEAD_DIM)

        a_out = latent_attention(q, k, v, k_c, v_c, attn_sink[l])
        cv_out = conv_module(u, w_dw[l], b_dw[l], ln_g[l], ln_b[l])
        x = x + gt1 * merge_groups(a_out, cv_out, g_attn_out[l], g_conv_out[l], w_out[l])

        h2 = modulate(rmsnorm(x, g_ffn[l]), sh2, sc2)
        x = x + gt2 * swiglu(h2, w_gate_up[l], w_down[l])

        if not last:
            a_c = context_attention(q_c.reshape(B, L, N_Q_HEADS, HEAD_DIM), k_c, v_c, attn_sink[l])
            cv_c = conv_module(u_c, w_dw[l], b_dw[l], ln_g[l], ln_b[l])
            ctx = ctx + cgt1 * merge_groups(a_c, cv_c, g_attn_out[l], g_conv_out[l], w_out[l])
            hc2 = modulate(rmsnorm(ctx, g_ffn[l]), csh2, csc2)
            ctx = ctx + cgt2 * swiglu(hc2, w_gate_up[l], w_down[l])
    return rmsnorm(x, g_final)


_drawn_inputs = setup_inputs


def setup_inputs(seed=0):
    import zlib

    import numpy as np

    out = dict(_drawn_inputs(seed))
    spreads = {}
    factors = {'attn_sink': 8.0, 'b_dw': 3.931, 'ln_b': 5.275}
    for name, (base, spread) in spreads.items():
        noise = np.random.default_rng([zlib.crc32(name.encode()), seed]).standard_normal(out[name].shape)
        drawn = base * np.exp(spread * noise) if base else spread * noise
        out[name] = __import__('jax').numpy.asarray(drawn.astype(out[name].dtype))
    for name, factor in factors.items():
        out[name] = (out[name] * factor).astype(out[name].dtype)
    return out
```

```python
import math
from contextlib import ExitStack

import numpy as np

import concourse.bass as bass
from concourse import mybir

F32, F32R, BF16 = mybir.dt.float32, mybir.dt.float32r, mybir.dt.bfloat16
ALU, ACT, AX = mybir.AluOpType, mybir.ActivationFunctionType, mybir.AxisListType

P = 128
D = 1024
DT = D // P
DEPTH = 2
N, L = 512, 256
T = N + L
TB, NB, LB = T // P, N // P, L // P
HEADS, KV, HD = 8, 2, 64
GRP = HEADS // KV
AW = HEADS * HD
CW = D - AW
CT = CW // P
TAPS = 31
PAD = TAPS // 2
D_FF = 2816
FT = D_FF // P
CHUNKS = (8, 8, 6)
GRID_W, FREQS = 64, HD // 4
EPS = 1e-6
SCALE = HD ** -0.5
MASKED = -1e30
MODS = 6
AG = 3
AGW = MODS * D // AG
ZW = PAD + N + 2 * PAD + L + PAD
CC = N + 2 * PAD
CVW = CC + L

OFF, n_ = {}, 0
for name_, width_ in (("b_ada", MODS * DT), ("g_mix", DT), ("g_ffn", DT), ("g_attn", CT), ("g_conv", CT),
                      ("b_dw", CT), ("ln_g", CT), ("ln_b", CT), ("w_dw", TAPS * CT), ("sink", HEADS)):
    OFF[name_] = n_
    n_ += width_
LAYER_COLS = n_
OFF["g_final"], OFF["cond"] = DEPTH * LAYER_COLS, DEPTH * LAYER_COLS + DT
COLS = DEPTH * LAYER_COLS + DT + 2 * DT

PHASES = [("u", 4, 8), ("qkv", 3, 8), ("oa", 2, 8), ("ob", 2, 8)]
for c_, k_ in enumerate(CHUNKS):
    PHASES += [(f"gu{c_}", k_, 8), (f"dn{c_}", 4, k_)]
PAIRS_OF = {name_: pairs_ for name_, pairs_, _ in PHASES}
FIRST, USES = {}, {}
n_ = m_ = 0
for l_ in range(DEPTH):
    for name_, pairs_, _k in PHASES:
        FIRST[l_, name_], USES[l_, name_] = n_, m_
        n_ += pairs_
        m_ += 4 if name_ in ("oa", "ob") else pairs_
PAIRS = n_
KTILES = [k for _l in range(DEPTH) for _n, pairs, k in PHASES for _p in range(pairs)]


def queries(layer):
    out = []
    for b in range(TB if layer == 0 else NB):
        keys = [NB, NB + 1] + ([t for t in (b - 1, b, b + 1) if 0 <= t < NB] if b < NB else [])
        out += [(g, b, keys) for g in range(KV)]
    return out


class Chain:

    def __init__(self, engine, sem):
        self.engine, self.sem, self.n = engine, sem, 0

    def link(self, instruction):
        instruction.then_inc(self.sem, 1)
        self.n += 1
        self.engine.wait_ge(self.sem, self.n)


def hybrid_backbone(nc, xT, params, w_ada, w_mix, w_out, w_gu, w_dn0, w_dn1, w_dn2,
                    rope, ident_in, masks_in, out):
    with ExitStack() as ctx:
        def sb(name, shape, dt=F32):
            return ctx.enter_context(nc.sbuf_tensor(name, shape, dt))

        def sem(name):
            return ctx.enter_context(nc.semaphore(name))

        x = sb("x", [P, DT, T])
        raw = [sb(f"raw{j}", [P, DT, P]) for j in range(2)]
        wH = [sb(f"w_high{j}", [P, DT, P], F32R) for j in range(2)]
        wL = [sb(f"w_low{j}", [P, DT, P], F32R) for j in range(2)]
        ada_raw = [sb(f"ada_raw{j}", [P, AGW]) for j in range(2)]
        ada_row = sb("ada_row", [P, AGW // 4])
        ssum = sb("ssum", [P, CVW])
        sq = [sb(f"sq{j}", [P, T]) for j in range(2)]
        tmp = [sb(f"tmp{j}", [P, T]) for j in range(2)]
        act_out = sb("act_out", [P, T])
        scratch = sb("diag_or_product", [P, CVW])
        diag = scratch[:, 0:T].rearrange("p (b t) -> p b t", t=P)
        par = sb("par", [P, COLS])
        mod = sb("mod", [P, DEPTH, MODS * DT, 2])
        gain = sb("gain", [P, DEPTH, 2, DT, 2])
        cond = sb("cond", [P, DT, 32])
        cosT = sb("cosT", [P, N])
        sinT = sb("sinT", [P, N])
        ident = sb("ident", [P, P])
        identb = sb("identb", [P, P], BF16)
        maskb = sb("maskb", [P, 2, P], BF16)
        mean_col = sb("mean_col", [P, 2])
        mean_all = sb("mean_all", [P, P])
        ones = sb("ones", [P, P])
        per_tok = sb("per_tok", [P, 2, TB])
        mx = sb("row_max", [P, 4])
        nmax = sb("neg_max", [P, 4])
        nsink = sb("nsink", [P, DEPTH, HEADS])
        esink = sb("esink", [P, 4])
        psums = sb("psums", [P, 4])
        eps = sb("eps", [P, 1])

        with ExitStack() as h_scope:
            hH = h_scope.enter_context(nc.sbuf_tensor("h_high", [P, DT, T], F32R))
            hL = h_scope.enter_context(nc.sbuf_tensor("h_low", [P, DT, T], F32R))
            with ExitStack() as s:
                z = s.enter_context(nc.sbuf_tensor("z_padded", [P, CT, ZW], F32))
                cv = s.enter_context(nc.sbuf_tensor("conv", [P, CT, CVW], F32))
                Q2 = s.enter_context(nc.sbuf_tensor("q_stacked", [P, HEADS, T], F32R))
                K2 = s.enter_context(nc.sbuf_tensor("k_stacked", [P, KV, 2, T], F32R))
            with ExitStack() as s:
                aH = s.enter_context(nc.sbuf_tensor("ff_high", [P, max(CHUNKS), T], F32R))
                aL = s.enter_context(nc.sbuf_tensor("ff_low", [P, max(CHUNKS), T], F32R))
        with ExitStack() as s:
            prob = s.enter_context(nc.sbuf_tensor("prob", [P, 2, 5 * P], F32))
            V2 = s.enter_context(nc.sbuf_tensor("v_stacked", [P, TB, KV, 2, HD], F32R))
            s.enter_context(nc.sbuf_tensor("gap", [P, 256], F32))
            aT = s.enter_context(nc.sbuf_tensor("attn_out", [P, CT, T], F32))
            PT = s.enter_context(nc.sbuf_tensor("probT", [P, 2, 5, GRP, P], F32R))

        bank = ctx.enter_context(nc.psum_tensor("banks", [P, 8, 512], F32))
        wide = bank[:].rearrange("p b n -> p (b n)")
        ADA, SMALL, BC, PTB = 4, 5, 6, 4

        par_in, x_in, const_in, mask_in = sem("par_in"), sem("x_in"), sem("const_in"), sem("mask_in")
        raw_in = [sem(f"raw_in{j}") for j in range(2)]
        ada_in = [sem(f"ada_in{j}") for j in range(2)]
        y_out = [sem(f"out_stored{j}") for j in range(2)]
        w_high, w_low = sem("w_high_ready"), sem("w_low_ready")
        gemm = sem("gemm_tile_done")
        slot_free = [sem(f"slot_read_out{j}") for j in range(2)]
        consts, cond_ok, casts_ok, nsink_ok = sem("constants_set"), sem("cond_ready"), sem("casts_ready"), sem("neg_sink_ready")
        ada_mm, ada_rowed = sem("ada_unit_done"), sem("ada_rows_copied")
        ada_tr, ada_cols = sem("ada_rows_transposed"), sem("ada_columns_ready")
        sum_ok, tok_mm, tok_root = sem("feature_sum_ready"), sem("token_mean_done"), sem("token_root_done")
        diag_ok, bc_ok = sem("diagonal_ready"), sem("stat_broadcast_done")
        sq_ok, sq_used = sem("square_ready"), sem("square_added")
        t_ok, high_ok, h_ok = sem("scaled_tile_ready"), sem("h_high_ready"), sem("h_tile_ready")
        conv_ok, zpad = sem("conv_tile_done"), sem("z_padding_zero")
        r_ok, qk_high, qk_ok = sem("rope_done"), sem("qk_high_ready"), sem("qk_ready")
        v_ok, v_tr, v_high, v_ready = sem("v_copied"), sem("v_transposed"), sem("v_high_ready"), sem("v_ready")
        s_ok, max_ok, exp_ok, prob_ok = sem("scores_done"), sem("max_ready"), sem("exp_ready"), sem("prob_ready")
        pt_ps, pt_high, pt_ok = sem("prob_transposed"), sem("probT_high_ready"), sem("probT_ready")
        pv_ok, pv_low, a_ok = sem("pv_done"), sem("pv_low_copied"), sem("attn_group_ready")
        ln_d, ln_y, ln_s = sem("conv_centred"), sem("conv_scaled"), sem("conv_silu_done")
        ff_high, ff_low = sem("ff_high_ready"), sem("ff_low_ready")
        y_ok = sem("out_tile_ready")
        dve_self, pool_self = sem("dve_self"), sem("pool_self")

        def col(name, i, layer=0):
            o = (layer * LAYER_COLS if name not in ("g_final", "cond") else 0) + OFF[name] + i
            return par[:, o:o + 1]

        def streams(layer, context=None):
            return [(0, N, 0)] + ([(N, T, 1)] if (layer == 0 if context is None else context) else [])

        STATS = [(l, s) for l in range(DEPTH) for s in ("n1", "an", "mean", "var", "cn", "n2")] + [(DEPTH, "n1")]
        stat_index = {s: i for i, s in enumerate(STATS)}
        root_index = {s: i for i, s in enumerate([s for s in STATS if s[1] != "mean"])}
        h_index, n = {}, 0
        for s in STATS[:-1]:
            if s[1] in ("n1", "an", "cn", "n2"):
                h_index[s] = n
                n += CT if s[1] in ("an", "cn") else DT
        sq_index, n = {}, 0
        for l in range(DEPTH):
            for s, tiles in [("x", DT)] * (l == 0) + [("an", CT), ("var", CT), ("cn", CT), ("ob", DT), ("dn2", DT)]:
                sq_index[l, s] = n
                n += tiles
        groups = [(l, q) for l in range(DEPTH) for q in range(len(queries(l)))]
        group_index = {g: i for i, g in enumerate(groups)}
        ADA_IN = {(0, "u"): 1, (0, "qkv"): 2, (0, "dn0"): 3, (0, "dn1"): 4, (0, "dn2"): 5}

        def ada_units(layer, name, block):
            if (layer, name) not in ADA_IN:
                return []
            last = 2 * PAIRS_OF[name] - 1
            return [(ADA_IN[layer, name], k) for k in range(DT) if k == block or (block == last and k > block)]

        POOL_TILES = (0, 3)
        DVE_TAPS = [(k, tap) for k in range(CT) if k not in POOL_TILES for tap in range(TAPS)]
        CONV_AFTER_U, CONV_AFTER_QKV = (0, 0, 14, 14), (5, 5, 6, 6, 6, TAPS)
        STAT_AFTER = {1: "mean", 4: "var", 7: "cn"}

        block = ctx.enter_context(nc.Block())

        @block.sync
        def _(sp):
            sp.dma_start(par[:], params).then_inc(par_in, 16)
            for k in range(DT):
                sp.dma_start(x[:, k, :], xT[k]).then_inc(x_in, 16)
                if k < 2:
                    sp.dma_start(ada_raw[k][:], w_ada[0, k]).then_inc(ada_in[k], 16)
            sp.dma_start(ident[:], ident_in).then_inc(const_in, 16)
            sp.dma_start(cosT[:], rope[0]).then_inc(const_in, 16)
            sp.dma_start(sinT[:], rope[1]).then_inc(const_in, 16)
            sp.dma_start(act_out[:, 0:2 * P], masks_in).then_inc(mask_in, 16)

            def load_ada(unit):
                i = unit[0] * DT + unit[1]
                sp.wait_ge(ada_mm, i - 1)
                sp.dma_start(ada_raw[i % 2][:], w_ada[unit[0], unit[1]]).then_inc(ada_in[i % 2], 16)

            for k in range(2, DT):
                load_ada((0, k))
            for layer in range(DEPTH):
                for name, pairs, ktiles in PHASES:
                    base = FIRST[layer, name]
                    src, skip = {"u": (w_mix, 0), "qkv": (w_mix, 4), "oa": (w_out, 0), "ob": (w_out, 2),
                                 "gu0": (w_gu, 0), "gu1": (w_gu, CHUNKS[0]), "gu2": (w_gu, CHUNKS[0] + CHUNKS[1]),
                                 "dn0": (w_dn0, 0), "dn1": (w_dn1, 0), "dn2": (w_dn2, 0)}[name]

                    def load_block(i, j):
                        sp.dma_start(raw[j][:, 0:ktiles, :],
                                     src[layer, j, i + skip].rearrange("p (k m) -> p k m", m=P)).then_inc(raw_in[j], 16)

                    if (layer, name) in ADA_IN:
                        for i in range(pairs):
                            for j in range(2):
                                if base + i > 0:
                                    sp.wait_ge(w_low, 2 * (base + i) + j - 1)
                                load_block(i, j)
                                for u in ada_units(layer, name, 2 * i + j):
                                    load_ada(u)
                    else:
                        with sp.Fori(0, pairs) as i:
                            for j in range(2):
                                sp.wait_ge(w_low, i * 2 + (2 * base + j - 1))
                                load_block(i, j)
            for k in range(DT):
                sp.wait_ge(y_ok, k + 1)
                sp.dma_start(out[k], tmp[k % 2][:, 0:N]).then_inc(y_out[k % 2], 16)
            for j in range(2):
                sp.wait_ge(y_out[j], 16 * DT // 2)

        @block.tensor
        def _(pe):
            mm = nc.tensor.matmul

            def ada_unit(unit):
                g, k = unit
                i = g * DT + k
                pe.wait_ge(ada_in[i % 2], 16 * (i // 2 + 1))
                for q in range(4):
                    last = mm(bank[32 * q:32 * q + 32, ADA, :], cond[:, k, :], ada_raw[i % 2][:, 512 * q:512 * q + 512],
                              start=(k == 0), stop=(k == DT - 1), tile_position=(0, 32 * q))
                last.then_inc(ada_mm, 1)

            def ada_turn(g):
                pe.wait_ge(ada_rowed, g + 1)
                for j in range(4):
                    last = nc.tensor.transpose(bank[:, SMALL, P * j:P * j + P], ada_row[:, P * j:P * j + P], ident[:])
                last.then_inc(ada_tr, 1)

            def stat(key, blocks):
                pe.wait_ge(sum_ok, stat_index[key] + 1)
                if key[1] == "mean":
                    lhs, lat, con = mean_all, ssum[:, 0:N], ssum[:, CC:CC + L]
                else:
                    width = mean_col[:, 0:1] if key[1] in ("n1", "n2") else mean_col[:, 1:2]
                    for b in range(blocks):
                        last = mm(bank[:, SMALL, b:b + 1], ssum[:, P * b:P * b + P], width, start=True, stop=True)
                    last.then_inc(tok_mm, 1)
                    pe.wait_ge(diag_ok, root_index[key] + 1)
                    lhs, lat, con = ones, scratch[:, 0:N], scratch[:, N:T]
                last = mm(bank[:, BC, 0:N], lhs[:], lat, start=True, stop=True)
                if blocks > NB:
                    last = mm(bank[:, BC + 1, 0:L], lhs[:], con, start=True, stop=True)
                last.then_inc(bc_ok, 1)

            def tile_product(w, k0_w, slot, ktiles, rhsH, rhsL, k0_rhs, ranges, ready=None):
                for k in range(ktiles):
                    if ready is not None:
                        pe.wait_ge(ready[0], ready[1] + k + 1)
                    for n, (weights, rhs) in enumerate(((wH, rhsH), (wH, rhsL), (wL, rhsH))):
                        for a, b in ranges:
                            last = mm(bank[:, 2 * slot + (a >= N), 0:b - a], weights[w][:, k0_w + k, :],
                                      rhs[:, k0_rhs + k, a:b], start=(k == 0 and n == 0),
                                      stop=(k == ktiles - 1 and n == 2))
                last.then_inc(gemm, 1)

            def gemm_block(layer, name, i, j, ktiles, rhsH, rhsL, ranges, ready=None):
                pe.wait_ge(w_low, i * 2 + (2 * FIRST[layer, name] + j + 1))
                if not isinstance(i, int) or USES[layer, name] + i > 0:
                    pe.wait_ge(slot_free[j], i + USES[layer, name])
                tile_product(j, 0, j, ktiles, rhsH, rhsL, 0, ranges, ready)

            def phase(layer, name, ktiles, rhsH, rhsL, ranges, ready=None):
                pairs = PAIRS_OF[name]
                with_ada = (layer, name) in ADA_IN
                for i in range(pairs if with_ada else 1):
                    for j in range(2):
                        gemm_block(layer, name, i, j, ktiles, rhsH, rhsL, ranges, ready if i + j == 0 else None)
                        for u in ada_units(layer, name, 2 * i + j):
                            ada_unit(u)
                if with_ada:
                    ada_turn(ADA_IN[layer, name])
                else:
                    with pe.Fori(1, pairs) as i:
                        for j in range(2):
                            gemm_block(layer, name, i, j, ktiles, rhsH, rhsL, ranges)

            def out_phase(layer, name, half, ranges, blocks):
                for t in range(DT):
                    i, j, m = t // 4, t // 2 % 2, t % 2
                    if m == 0:
                        pe.wait_ge(w_low, 2 * (FIRST[layer, name] + i) + j + 1)
                    if t >= 2 or half:
                        pe.wait_ge(slot_free[m], USES[layer, name] + t // 2)
                    tile_product(j, 4 * m, m, CT, hH, hL, CT * half, ranges,
                                 (h_ok, h_index[layer, "cn" if half else "an"]) if t == 0 else None)
                    if not half and t in STAT_AFTER:
                        stat((layer, STAT_AFTER[t]), blocks)

            def attention(layer):
                qs = queries(layer)
                order = [(q, i) for q in range(len(qs)) for i in range(GRP)]
                unit0 = GRP * group_index[layer, 0]

                def scores(n):
                    q, i = order[n]
                    g, b, keys = qs[q]
                    u = unit0 + n
                    if n == 0:
                        pe.wait_ge(qk_ok, 5 * (layer + 1))
                        for j in range(2):
                            pe.wait_ge(slot_free[j], USES[layer, "oa"])
                    if u >= 2:
                        pe.wait_ge(exp_ok, u - 1)
                    s = 1024 * (u % 2)
                    window = keys[2:]
                    spans = [(0, N, 2 * P)]
                    if window:
                        spans.append((2 * P, P * window[0], P * min(2, len(window))))
                    if len(window) == 3:
                        spans.append((4 * P, P * window[2], P))
                    parts = [(at, w, Q2[:, g * GRP + i, P * b:P * b + P], K2[:, g, part, tok:tok + w])
                             for at, tok, w in spans for part in range(2)]
                    parts += [((2 + m) * P, P, identb[:], maskb[:, 0 if t < b else 1, :])
                              for m, t in enumerate(window) if t != b]
                    in_bank = [at // 512 for at, *_ in parts]
                    for m, (at, w, lhs, rhs) in enumerate(parts):
                        last = mm(wide[:, s + at:s + at + w], lhs, rhs, start=in_bank[m] not in in_bank[:m],
                                  stop=in_bank[m] not in in_bank[m + 1:], skip_group_check=True)
                    last.then_inc(s_ok, 1)

                def turn(n):
                    u, keys = unit0 + n, qs[order[n][0]][2]
                    pe.wait_ge(prob_ok, u + 1)
                    if n:
                        pe.wait_ge(pt_ok, u)
                    else:
                        pe.wait_ge(v_ready, layer + 1)
                    for m in range(len(keys)):
                        last = nc.tensor.transpose(wide[:, 512 * PTB + P * m:512 * PTB + P * m + P],
                                                   prob[:, u % 2, P * m:P * m + P], ident[:])
                    last.then_inc(pt_ps, 1)

                def values(q):
                    g, b, keys = qs[q]
                    gi = group_index[layer, q]
                    pe.wait_ge(pt_ok, GRP * gi + GRP)
                    if gi >= 2:
                        pe.wait_ge(a_ok, gi - 1)
                    for m, t in enumerate(keys):
                        for part in range(2):
                            last = mm(bank[:, BC + gi % 2, :], V2[:, t, g, :, :].rearrange("p a d -> p (a d)"),
                                      PT[:, part, m, :, :].rearrange("p h q -> p (h q)"),
                                      start=(m == 0 and part == 0), stop=(m == len(keys) - 1 and part == 1))
                    last.then_inc(pv_ok, 1)

                pe.wait_ge(v_ok, layer + 1)
                if layer == 0:
                    pe.wait_ge(ada_cols, 3)
                for b in range(TB):
                    last = nc.tensor.transpose(wide[:, 512 * PTB + P * b:512 * PTB + P * b + P],
                                               tmp[1][:, P * b:P * b + P], ident[:])
                last.then_inc(v_tr, 1)
                scores(0)
                for n in range(len(order)):
                    if n + 1 < len(order):
                        scores(n + 1)
                    if n and n % GRP == 0:
                        values(n // GRP - 1)
                    turn(n)
                values(len(qs) - 1)

            pe.wait_ge(consts, 4)
            pe.wait_ge(const_in, 48)
            pe.wait_ge(cond_ok, 1)
            stat((0, "n1"), TB)
            for k in range(DT):
                ada_unit((0, k))
            ada_turn(0)
            for layer in range(DEPTH):
                ranges = [(a, b) for a, b, _ in streams(layer)]
                blocks = TB if layer == 0 else NB
                if layer:
                    pe.wait_ge(ada_cols, AG * DEPTH)
                    stat((layer, "n1"), TB)
                phase(layer, "u", DT, hH, hL, ranges, (h_ok, h_index[layer, "n1"]))
                for i in range(PAIRS_OF["qkv"]):
                    for j in range(2):
                        gemm_block(layer, "qkv", i, j, DT, hH, hL, [(0, N), (N, T)] if i == 2 else ranges)
                        for u in ada_units(layer, "qkv", 2 * i + j):
                            ada_unit(u)
                if (layer, "qkv") in ADA_IN:
                    ada_turn(ADA_IN[layer, "qkv"])
                attention(layer)
                stat((layer, "an"), blocks)
                out_phase(layer, "oa", 0, ranges, blocks)
                out_phase(layer, "ob", 1, ranges, blocks)
                stat((layer, "n2"), blocks)
                for c, tiles in enumerate(CHUNKS):
                    phase(layer, f"gu{c}", DT, hH, hL, ranges, (h_ok, h_index[layer, "n2"]) if c == 0 else None)
                    phase(layer, f"dn{c}", tiles, aH, aL, ranges, (ff_low, layer * FT + sum(CHUNKS[:c])))
            stat((DEPTH, "n1"), NB)

        @block.scalar
        def _(act):
            f = nc.scalar.activation

            def split_high(layer, name, i, j, last_pair):
                p = FIRST[layer, name] + (last_pair if isinstance(i, int) else 0)
                step = 4 if name in ("oa", "ob") else 2
                done = 2 * USES[layer, name] + (2 * j + 2 if step == 4 else j + 1)
                act.wait_ge(gemm, i * step + done)
                act.wait_ge(raw_in[j], i * 16 + 16 * (FIRST[layer, name] + 2))
                k = ktiles_after(layer, name, i)
                f(wH[j][:, 0:k, :], raw[j][:, 0:k, :], ACT.Copy).then_inc(w_high, 1)

            def first_high():
                for j in range(2):
                    act.wait_ge(raw_in[j], 16)
                    f(wH[j][:], raw[j][:], ACT.Copy).then_inc(w_high, 1)

            def square(series, layer, k, src):
                n = sq_index[layer, series] + k
                if n >= 2:
                    act.wait_ge(sq_used, n - 1)
                w = src.shape[-1]
                f(sq[n % 2][:, 0:w], src, ACT.Square).then_inc(sq_ok, 1)

            def root(key, blocks):
                act.wait_ge(tok_mm, root_index[key] + 1)
                f(per_tok[:, 0, 0:blocks], bank[:, SMALL, 0:blocks], ACT.Sqrt, bias=eps[:]).then_inc(tok_root, 1)

            def high(key, k0, tiles, layer, shift=None, width=T):
                for k in range(tiles):
                    act.wait_ge(t_ok, h_index[key] + k + 1)
                    if shift is None:
                        f(hH[:, k0 + k, 0:width], tmp[k % 2][:, 0:width], ACT.Copy).then_inc(high_ok, 1)
                        continue
                    for a, b, v in streams(layer, width > N):
                        last = f(hH[:, k, a:b], tmp[k % 2][:, a:b], ACT.Identity,
                                 bias=mod[:, layer, shift * DT + k, v:v + 1])
                    last.then_inc(high_ok, 1)

            def ada_rows(g):
                act.wait_ge(ada_mm, DT * (g + 1))
                if g:
                    act.wait_ge(ada_tr, g)
                f(ada_row[:], bank[:, ADA, :], ACT.Copy).then_inc(ada_rowed, 1)

            def ada_after(layer, name):
                if (layer, name) in ADA_IN:
                    ada_rows(ADA_IN[layer, name])

            def attention(layer):
                qs = queries(layer)
                order = [(q, i) for q in range(len(qs)) for i in range(GRP)]
                unit0 = GRP * group_index[layer, 0]

                def pv_copy(q):
                    gi = group_index[layer, q]
                    act.wait_ge(pv_ok, gi + 1)
                    if q:
                        act.wait_ge(a_ok, gi)
                    f(act_out[0:HD, 0:GRP * P], bank[HD:P, BC + gi % 2, :], ACT.Copy).then_inc(pv_low, 1)

                def prob_high(n):
                    u, (q, i) = unit0 + n, order[n]
                    if n and i == 0:
                        pv_copy(q - 1)
                    w = len(qs[q][2])
                    act.wait_ge(pt_ps, u + 1)
                    f(PT[:, 0, 0:w, i, :], wide[:, 512 * PTB:512 * PTB + P * w].rearrange("p (k q) -> p k q", k=w),
                      ACT.Copy).then_inc(pt_high, 1)

                act.wait_ge(v_tr, layer + 1)
                f(V2[:, :, :, 0, :], wide[:, 512 * PTB:512 * PTB + T].rearrange("p (t g d) -> p t g d", t=TB, g=KV),
                  ACT.Copy).then_inc(v_high, 1)
                for n in range(len(order)):
                    u, (q, i) = unit0 + n, order[n]
                    w = P * len(qs[q][2])
                    act.wait_ge(max_ok, u + 1)
                    if u >= 2:
                        act.wait_ge(pt_ps, u - 1)
                    f(prob[:, u % 2, 0:w], wide[:, 1024 * (u % 2):1024 * (u % 2) + w], ACT.Exp,
                      bias=nmax[:, u % 4:u % 4 + 1], scale=SCALE, accum_out=psums[:, u % 4:u % 4 + 1])
                    f(esink[:, u % 4:u % 4 + 1], col("sink", qs[q][0] * GRP + i, layer), ACT.Exp,
                      bias=nmax[:, u % 4:u % 4 + 1]).then_inc(exp_ok, 1)
                    if n:
                        prob_high(n - 1)
                prob_high(len(order) - 1)
                pv_copy(len(qs) - 1)

            act.wait_ge(par_in, 16)
            act.wait_ge(consts, 4)
            f(cond[:, :, 0:2], par[:, OFF["cond"]:OFF["cond"] + 2 * DT].rearrange("p (k v) -> p k v", v=2),
              ACT.Silu).then_inc(cond_ok, 1)
            act.wait_ge(x_in, 16 * DT)
            for k in range(DT):
                square("x", 0, k, x[:, k, :])
            act.wait_ge(const_in, 48)
            f(identb[:], ident[:], ACT.Copy)
            act.wait_ge(mask_in, 16)
            f(maskb[:].rearrange("p m t -> p (m t)"), act_out[:, 0:2 * P], ACT.Copy).then_inc(casts_ok, 1)
            act.wait_ge(casts_ok, 1)
            root((0, "n1"), TB)
            ada_rows(0)
            first_high()
            for layer in range(DEPTH):
                width, blocks = (T, TB) if layer == 0 else (N, NB)
                if layer:
                    root((layer, "n1"), TB)
                high((layer, "n1"), 0, DT, layer, shift=0)

                def u_pair(i):
                    split_high(layer, "u", i, 0, 0)
                    split_high(layer, "u", i, 1, 0)
                    if not isinstance(i, int) or USES[layer, "u"] + i > 0:
                        act.wait_ge(slot_free[0], i + USES[layer, "u"])
                    f(act_out[:, 0:width], wide[:, 1024:1024 + width], ACT.Sigmoid).then_inc(slot_free[1], 1)

                u_pair(0)
                with act.Fori(1, PAIRS_OF["u"]) as i:
                    u_pair(i)
                ada_after(layer, "u")

                for i in range(3):
                    for j in range(2):
                        split_high(layer, "qkv", i, j, 0)
                        t = 2 * i + j
                        if t < 4:
                            act.wait_ge(r_ok, 5 * layer + t + 1)
                            f(Q2[0:HD, 2 * t, 0:width], tmp[j][0:HD, 0:width], ACT.Copy)
                            f(Q2[HD:P, 2 * t + 1, 0:width], tmp[j][HD:P, 0:width], ACT.Copy).then_inc(qk_high, 1)
                        elif t == 4:
                            act.wait_ge(r_ok, 5 * layer + t + 1)
                            for g in range(KV):
                                for half in range(2):
                                    last = f(K2[HD * half:HD * half + HD, g, 0, :], tmp[0][HD * g:HD * g + HD, :], ACT.Copy)
                            last.then_inc(qk_high, 1)
                        else:
                            act.wait_ge(qk_ok, 5 * layer + 4)
                            f(tmp[1][:], wide[:, 1024:1024 + T], ACT.Copy).then_inc(v_ok, 1)
                ada_after(layer, "qkv")
                attention(layer)

                act.wait_ge(a_ok, group_index[layer, len(queries(layer)) - 1] + 1)
                for k in range(CT):
                    square("an", layer, k, aT[:, k, 0:width])
                root((layer, "an"), blocks)
                high((layer, "an"), 0, CT, layer, width=width)
                for t in range(DT):
                    if t % 2:
                        split_high(layer, "oa", t // 4, t // 2 % 2, 0)
                    if t == 1:
                        for k in range(CT):
                            act.wait_ge(ln_d, CT * layer + k + 1)
                            square("var", layer, k, z[:, k, 0:width])
                    if t == 3:
                        root((layer, "var"), blocks)
                    if t == 5:
                        for k in range(CT):
                            act.wait_ge(ln_y, CT * layer + k + 1)
                            f(cv[:, k, 0:width], tmp[k % 2][:, 0:width], ACT.Silu,
                              bias=col("ln_b", k, layer)).then_inc(ln_s, 1)
                            act.wait_ge(ln_s, CT * layer + k + 1)
                            square("cn", layer, k, cv[:, k, 0:width])
                root((layer, "cn"), blocks)
                high((layer, "cn"), CT, CT, layer, width=width)
                for t in range(DT):
                    if t % 2:
                        split_high(layer, "ob", t // 4, t // 2 % 2, 0)
                    act.wait_ge(slot_free[t % 2], USES[layer, "ob"] + t // 2 + 1)
                    square("ob", layer, t, x[:, t, 0:width])
                root((layer, "n2"), blocks)
                high((layer, "n2"), 0, DT, layer, shift=3, width=width)

                for c, tiles in enumerate(CHUNKS):
                    gu, dn = f"gu{c}", f"dn{c}"

                    def gu_pair(i):
                        split_high(layer, gu, i, 0, 0)
                        act.wait_ge(slot_free[1], i + USES[layer, gu])
                        f(act_out[:, 0:width], wide[:, 0:width], ACT.Silu).then_inc(slot_free[0], 1)
                        split_high(layer, gu, i, 1, 0)
                        act.wait_ge(slot_free[1], i + (USES[layer, gu] + 1))
                        f(aH[:, i, 0:width], tmp[0][:, 0:width], ACT.Copy).then_inc(ff_high, 1)

                    with act.Fori(0, tiles - 1) as i:
                        gu_pair(i)
                    gu_pair(tiles - 1)

                    def dn_pair(i, more=True):
                        for j in range(2):
                            if more:
                                split_high(layer, dn, i, j, 0)
                            if c == 2:
                                n = sq_index[layer, "dn2"]
                                act.wait_ge(slot_free[j], i + (USES[layer, dn] + 1))
                                act.wait_ge(sq_used, i * 2 + (n + j - 1))
                                f(sq[j][:, 0:width], x[:, i * 2 + j, 0:width], ACT.Square).then_inc(sq_ok, 1)

                    with act.Fori(0, PAIRS_OF[dn] - 1) as i:
                        dn_pair(i)
                    dn_pair(PAIRS_OF[dn] - 1, more=(layer, c) != (DEPTH - 1, 2))
                    ada_after(layer, dn)
            root((DEPTH, "n1"), NB)

        @block.vector
        def _(dve):
            chain = Chain(dve, dve_self)
            tt, stt, ts = nc.vector.tensor_tensor, nc.vector.scalar_tensor_tensor, nc.vector.tensor_scalar

            def f32(ap):
                return ap.bitcast(F32)

            def split_low(layer, name, i, j):
                dve.wait_ge(w_high, i * 2 + (2 * FIRST[layer, name] + j + 3))
                k = ktiles_after(layer, name, i)
                tt(wL[j][:, 0:k, :], raw[j][:, 0:k, :], f32(wH[j][:, 0:k, :]), ALU.subtract).then_inc(w_low, 1)

            def add_square(series, layer, k, width):
                n = sq_index[layer, series] + k
                dve.wait_ge(sq_ok, n + 1)
                if k:
                    dve.wait_ge(sq_used, n)
                    tt(ssum[:, 0:width], ssum[:, 0:width], sq[n % 2][:, 0:width], ALU.add).then_inc(sq_used, 1)
                else:
                    nc.vector.tensor_copy(ssum[:, 0:width], sq[n % 2][:, 0:width]).then_inc(sq_used, 1)

            def sum_done(series, layer, tiles):
                dve.wait_ge(sq_used, sq_index[layer, series] + tiles)
                nc.vector.tensor_copy(mx[:, 0:1], ssum[:, 0:1]).then_inc(sum_ok, 1)

            def diagonal(key, blocks):
                n = root_index[key] + 1
                dve.wait_ge(tok_root, n)
                chain.link(nc.vector.reciprocal(per_tok[:, 1, 0:blocks], per_tok[:, 0, 0:blocks]))
                for b in range(blocks):
                    last = ts(diag[:, b, :], ident[:], per_tok[:, 1, b:b + 1], None, ALU.mult)
                last.then_inc(diag_ok, 1)
                dve.wait_ge(bc_ok, stat_index[key] + 1)

            def normalise(key, src, scale, k0, tiles, layer, shift=None, width=T):
                base = h_index[key]

                def low(k):
                    dve.wait_ge(high_ok, base + k + 1)
                    t = tmp[k % 2]
                    if shift is None:
                        last = tt(hL[:, k0 + k, 0:width], t[:, 0:width], f32(hH[:, k0 + k, 0:width]), ALU.subtract)
                    else:
                        for a, b, v in streams(layer, width > N):
                            last = stt(out=hL[:, k, a:b], in0=t[:, a:b], scalar=mod[:, layer, shift * DT + k, v:v + 1],
                                       in1=f32(hH[:, k, a:b]), op0=ALU.add, op1=ALU.subtract)
                    last.then_inc(h_ok, 1)

                for k in range(tiles):
                    if base + k > 1:
                        dve.wait_ge(h_ok, base + max(k - 1, 0))
                    for a, b, s in scale(k):
                        last = stt(out=tmp[k % 2][:, a:b], in0=src(k)[:, a:b], scalar=s,
                                   in1=wide[:, 512 * BC + a:512 * BC + b], op0=ALU.mult, op1=ALU.mult)
                    last.then_inc(t_ok, 1)
                    if k:
                        low(k - 1)
                low(tiles - 1)

            def modulated(layer, which, width):
                return lambda k: [(a, b, gain[:, layer, which, k, v:v + 1]) for a, b, v in streams(layer, width > N)]

            def ada_columns(g):
                layer, gg = g // AG, g % AG
                dve.wait_ge(ada_tr, g + 1)
                for v in range(2):
                    src = bank[:, SMALL, :].rearrange("p (j q z) -> p q j z", q=4, z=32)[:, :, :, v]
                    dst = mod[:, layer, 16 * gg:16 * gg + 16, v].rearrange("p (q j) -> p q j", q=4)
                    o = layer * LAYER_COLS + OFF["b_ada"] + 16 * gg
                    last = tt(dst, src, par[:, o:o + 16].rearrange("p (q j) -> p q j", q=4), ALU.add)
                chain.link(last)
                if gg != 1:
                    which = gg // 2
                    vec = 1 if gg == 0 else 4
                    o = layer * LAYER_COLS + OFF["g_mix" if which == 0 else "g_ffn"]
                    for v in range(2):
                        last = stt(out=gain[:, layer, which, :, v], in0=mod[:, layer, vec * DT:(vec + 1) * DT, v],
                                   scalar=1.0, in1=par[:, o:o + DT], op0=ALU.add, op1=ALU.mult)
                    chain.link(last)
                nc.vector.tensor_copy(mx[:, 1:2], mod[:, layer, 16 * gg, 0:1]).then_inc(ada_cols, 1)

            def ada_after(layer, name):
                if (layer, name) in ADA_IN:
                    ada_columns(ADA_IN[layer, name])

            def update(layer, slot, use, gate, t, ranges):
                dve.wait_ge(slot_free[slot], use)
                for a, b, v in ranges:
                    xt = x[:, t, a:b]
                    last = stt(out=xt, in0=bank[:, 2 * slot + (a >= N), 0:b - a],
                               scalar=mod[:, layer, bass.ds(t + gate * DT, 1), v], in1=xt, op0=ALU.mult, op1=ALU.add)
                last.then_inc(slot_free[slot], 1)

            def attention(layer):
                qs = queries(layer)
                order = [(q, i) for q in range(len(qs)) for i in range(GRP)]
                unit0 = GRP * group_index[layer, 0]

                def row_max(n):
                    u, (q, i) = unit0 + n, order[n]
                    w, c = P * len(qs[q][2]), u % 4
                    dve.wait_ge(s_ok, u + 1)
                    chain.link(nc.vector.reduce_max(mx[:, c:c + 1], wide[:, 1024 * (u % 2):1024 * (u % 2) + w], AX.X))
                    h = qs[q][0] * GRP + i
                    ts(nmax[:, c:c + 1], mx[:, c:c + 1], -SCALE, nsink[:, layer, h:h + 1], ALU.mult, ALU.min)\
                        .then_inc(max_ok, 1)

                def divide(n):
                    u, w = unit0 + n, P * len(qs[order[n][0]][2])
                    c = u % 4
                    dve.wait_ge(exp_ok, u + 1)
                    chain.link(tt(psums[:, c:c + 1], psums[:, c:c + 1], esink[:, c:c + 1], ALU.add))
                    chain.link(nc.vector.reciprocal(psums[:, c:c + 1], psums[:, c:c + 1]))
                    ts(prob[:, u % 2, 0:w], prob[:, u % 2, 0:w], psums[:, c:c + 1], None, ALU.mult).then_inc(prob_ok, 1)

                def combine(q):
                    g, b, _ = qs[q]
                    gi = group_index[layer, q]
                    dve.wait_ge(pv_low, gi + 1)
                    for par_ in range(2):
                        halves = [ap.rearrange("p (i two t) -> p i two t", two=2, t=P)[:, :, par_, :]
                                  for ap in (bank[0:HD, BC + gi % 2, :], act_out[0:HD, 0:GRP * P])]
                        last = tt(aT[HD * par_:HD * par_ + HD, 2 * g:2 * g + 2, P * b:P * b + P], *halves, ALU.add)
                    last.then_inc(a_ok, 1)

                def prob_low(n):
                    u, (q, i) = unit0 + n, order[n]
                    if n and i == 0:
                        combine(q - 1)
                    w = len(qs[q][2])
                    dve.wait_ge(pt_high, u + 1)
                    tt(PT[:, 1, 0:w, i, :], wide[:, 512 * PTB:512 * PTB + P * w].rearrange("p (k q) -> p k q", k=w),
                       f32(PT[:, 0, 0:w, i, :]), ALU.subtract).then_inc(pt_ok, 1)

                dve.wait_ge(v_high, layer + 1)
                tt(V2[:, :, :, 1, :], wide[:, 512 * PTB:512 * PTB + T].rearrange("p (t g d) -> p t g d", t=TB, g=KV),
                   f32(V2[:, :, :, 0, :]), ALU.subtract).then_inc(v_ready, 1)
                for n in range(len(order) + 2):
                    if n < len(order):
                        row_max(n)
                    if 1 <= n <= len(order):
                        divide(n - 1)
                    if n >= 2:
                        prob_low(n - 2)
                combine(len(qs) - 1)

            def rope(layer, t, j, context):
                dve.wait_ge(gemm, 2 * USES[layer, "qkv"] + t + 1)
                if layer + t:
                    dve.wait_ge(r_ok, 5 * layer + t)
                r, rot = tmp[j], sq[0]
                nc.vector.stream_shuffle(rot[:, 0:N], bank[:, 2 * j, :], [(m + FREQS) % 32 for m in range(32)])
                if context:
                    nc.vector.tensor_copy(r[:, N:T], bank[:, 2 * j + 1, 0:L])
                tt(r[:, 0:N], bank[:, 2 * j, :], cosT[:], ALU.mult).then_inc(slot_free[j], 1)
                dve.wait_ge(slot_free[j], USES[layer, "qkv"] + t // 2 + 1)
                chain.link(tt(rot[:, 0:N], rot[:, 0:N], sinT[:], ALU.mult))
                tt(r[:, 0:N], r[:, 0:N], rot[:, 0:N], ALU.add).then_inc(r_ok, 1)

            dve.wait_ge(par_in, 16)
            for layer in range(DEPTH):
                o = layer * LAYER_COLS + OFF["sink"]
                ts(nsink[:, layer, :], par[:, o:o + HEADS], -1.0, None, ALU.mult).then_inc(nsink_ok, 1)
            for k in range(DT):
                add_square("x", 0, k, T)
            sum_done("x", 0, DT)
            dve.wait_ge(const_in, 48)
            dve.wait_ge(nsink_ok, DEPTH)
            diagonal((0, "n1"), TB)
            ada_columns(0)
            for j in range(2):
                dve.wait_ge(w_high, j + 1)
                tt(wL[j][:], raw[j][:], f32(wH[j][:]), ALU.subtract).then_inc(w_low, 1)
            for layer in range(DEPTH):
                width, blocks = (T, TB) if layer == 0 else (N, NB)
                now = streams(layer)
                if layer:
                    diagonal((layer, "n1"), TB)
                normalise((layer, "n1"), lambda k: x[:, k, :], modulated(layer, 0, T), 0, DT, layer, shift=0)

                def u_pair(i):
                    split_low(layer, "u", i, 0)
                    split_low(layer, "u", i, 1)
                    dve.wait_ge(slot_free[1], i + (USES[layer, "u"] + 1))
                    for a, b, _v in now:
                        at = PAD if a == 0 else CC + PAD
                        last = tt(z[:, i, at:at + b - a], bank[:, a // N, 0:b - a], act_out[:, a:b], ALU.mult)
                    last.then_inc(slot_free[0], 1)

                cw = CVW if layer == 0 else N
                taps = list(DVE_TAPS)

                def convolve(n):
                    for _ in range(min(n, len(taps))):
                        k, tap = taps.pop(0)
                        acc, src, w = cv[:, k, 0:cw], z[:, k, tap:tap + cw], col("w_dw", tap * CT + k, layer)
                        if tap == 0:
                            dve.wait_ge(zpad, layer + 1)
                            dve.wait_ge(slot_free[0], USES[layer, "u"] + k + 1)
                            chain.link(ts(acc, src, w, col("b_dw", k, layer), ALU.mult, ALU.add))
                        else:
                            chain.link(stt(out=acc, in0=src, scalar=w, in1=acc, op0=ALU.mult, op1=ALU.add))

                for i in range(PAIRS_OF["u"]):
                    u_pair(i)
                    convolve(CONV_AFTER_U[i])
                ada_after(layer, "u")

                for i in range(3):
                    for j in range(2):
                        split_low(layer, "qkv", i, j)
                        t = 2 * i + j
                        if t < 4:
                            rope(layer, t, j, layer == 0)
                            dve.wait_ge(qk_high, 5 * layer + t + 1)
                            tt(Q2[HD:P, 2 * t, 0:width], tmp[j][0:HD, 0:width], f32(Q2[0:HD, 2 * t, 0:width]), ALU.subtract)
                            tt(Q2[0:HD, 2 * t + 1, 0:width], tmp[j][HD:P, 0:width], f32(Q2[HD:P, 2 * t + 1, 0:width]),
                               ALU.subtract).then_inc(qk_ok, 1)
                        elif t == 4:
                            rope(layer, t, j, True)
                            dve.wait_ge(qk_high, 5 * layer + t + 1)
                            for g in range(KV):
                                for half in range(2):
                                    last = tt(K2[HD * half:HD * half + HD, g, 1, :], tmp[0][HD * g:HD * g + HD, :],
                                              f32(K2[HD * g:HD * g + HD, g, 0, :]), ALU.subtract)
                            last.then_inc(qk_ok, 1)
                        else:
                            dve.wait_ge(v_ok, layer + 1)
                            nc.vector.tensor_copy(mx[:, 0:1], tmp[1][:, 0:1]).then_inc(slot_free[1], 1)
                        convolve(CONV_AFTER_QKV[t])
                ada_after(layer, "qkv")
                attention(layer)

                for k in range(CT):
                    add_square("an", layer, k, width)
                sum_done("an", layer, CT)
                dve.wait_ge(conv_ok, len(POOL_TILES) * (layer + 1))
                diagonal((layer, "an"), blocks)
                normalise((layer, "an"), lambda k: aT[:, k, :], lambda k: [(0, width, col("g_attn", k, layer))],
                          0, CT, layer, width=width)

                chain.link(tt(ssum[:, 0:cw], cv[:, 0, 0:cw], cv[:, 1, 0:cw], ALU.add))
                chain.link(tt(ssum[:, 0:cw], ssum[:, 0:cw], cv[:, 2, 0:cw], ALU.add))
                tt(ssum[:, 0:cw], ssum[:, 0:cw], cv[:, 3, 0:cw], ALU.add).then_inc(sum_ok, 1)
                for t in range(DT):
                    if t % 2:
                        split_low(layer, "oa", t // 4, t // 2 % 2)
                    dve.wait_ge(gemm, 2 * USES[layer, "oa"] + t + 1)
                    update(layer, t % 2, USES[layer, "oa"] + t // 2, 2, t, now)
                    if t == 1:
                        dve.wait_ge(bc_ok, stat_index[layer, "mean"] + 1)
                        for k in range(CT):
                            for a, b, _v in now:
                                at = a if a == 0 else CC
                                last = tt(z[:, k, a:b], cv[:, k, at:at + b - a], wide[:, 512 * BC + a:512 * BC + b], ALU.subtract)
                            last.then_inc(ln_d, 1)
                        for k in range(CT):
                            add_square("var", layer, k, width)
                        sum_done("var", layer, CT)
                    if t == 4:
                        diagonal((layer, "var"), blocks)
                    if t == 5:
                        for k in range(CT):
                            if k >= 2:
                                dve.wait_ge(ln_s, CT * layer + k - 1)
                            stt(out=tmp[k % 2][:, 0:width], in0=z[:, k, 0:width], scalar=col("ln_g", k, layer),
                                in1=wide[:, 512 * BC:512 * BC + width], op0=ALU.mult, op1=ALU.mult).then_inc(ln_y, 1)
                        for k in range(CT):
                            add_square("cn", layer, k, width)
                        sum_done("cn", layer, CT)
                diagonal((layer, "cn"), blocks)
                normalise((layer, "cn"), lambda k: cv[:, k, :], lambda k: [(0, width, col("g_conv", k, layer))],
                          CT, CT, layer, width=width)

                for t in range(DT):
                    if t % 2:
                        split_low(layer, "ob", t // 4, t // 2 % 2)
                    dve.wait_ge(gemm, 2 * USES[layer, "ob"] + t + 1)
                    update(layer, t % 2, USES[layer, "ob"] + t // 2, 2, t, now)
                    add_square("ob", layer, t, width)
                sum_done("ob", layer, DT)
                diagonal((layer, "n2"), blocks)
                normalise((layer, "n2"), lambda k: x[:, k, :], modulated(layer, 1, width), 0, DT, layer, shift=3, width=width)

                for c, tiles in enumerate(CHUNKS):
                    gu, dn = f"gu{c}", f"dn{c}"
                    ff = layer * FT + sum(CHUNKS[:c])

                    def gu_pair(i):
                        split_low(layer, gu, i, 0)
                        split_low(layer, gu, i, 1)
                        dve.wait_ge(ff_low, i + ff)
                        dve.wait_ge(slot_free[0], i + (USES[layer, gu] + 1))
                        tt(tmp[0][:, 0:width], wide[:, 1024:1024 + width], act_out[:, 0:width], ALU.mult)\
                            .then_inc(slot_free[1], 1)
                        dve.wait_ge(ff_high, i + (ff + 1))
                        tt(aL[:, i, 0:width], tmp[0][:, 0:width], f32(aH[:, i, 0:width]), ALU.subtract).then_inc(ff_low, 1)

                    with dve.Fori(0, tiles - 1) as i:
                        gu_pair(i)
                    gu_pair(tiles - 1)

                    def dn_pair(i, more=True):
                        for j in range(2):
                            if more:
                                split_low(layer, dn, i, j)
                            dve.wait_ge(gemm, i * 2 + (2 * USES[layer, dn] + j + 1))
                            update(layer, j, i + USES[layer, dn], 5, i * 2 + j, now)
                            if c == 2:
                                n = sq_index[layer, "dn2"]
                                dve.wait_ge(sq_ok, i * 2 + (n + j + 1))
                                dve.wait_ge(sq_used, i * 2 + (n + j))
                                tt(ssum[:, 0:width], ssum[:, 0:width], sq[j][:, 0:width], ALU.add).then_inc(sq_used, 1)

                    if c == 2:
                        chain.link(nc.vector.memset(ssum[:, 0:width], 0.0))
                    with dve.Fori(0, PAIRS_OF[dn] - 1) as i:
                        dn_pair(i)
                    dn_pair(PAIRS_OF[dn] - 1, more=(layer, c) != (DEPTH - 1, 2))
                    if c == 2:
                        sum_done("dn2", layer, DT)
                    ada_after(layer, dn)
            diagonal((DEPTH, "n1"), NB)
            for k in range(DT):
                if k >= 2:
                    dve.wait_ge(y_out[k % 2], 16 * (k // 2))
                stt(out=tmp[k % 2][:, 0:N], in0=x[:, k, 0:N], scalar=col("g_final", k), in1=wide[:, 512 * BC:512 * BC + N],
                    op0=ALU.mult, op1=ALU.mult).then_inc(y_ok, 1)

        @block.gpsimd
        def _(pool):
            chain = Chain(pool, pool_self)
            nc.gpsimd.memset(cond[:], 0.0).then_inc(consts, 1)
            nc.gpsimd.memset(eps[:], EPS).then_inc(consts, 1)
            nc.gpsimd.memset(ones[:], 1.0)
            nc.gpsimd.memset(mean_all[:], 1.0 / CW).then_inc(consts, 1)
            nc.gpsimd.memset(mean_col[:, 0:1], 1.0 / D)
            nc.gpsimd.memset(mean_col[:, 1:2], 1.0 / CW).then_inc(consts, 1)
            pool.wait_ge(par_in, 16)
            for layer in range(DEPTH):
                if layer:
                    pool.wait_ge(gemm, 2 * USES[layer, "u"])
                pads = [(0, PAD), (PAD + N, PAD + N + 2 * PAD), (ZW - PAD, ZW)][:3 if layer == 0 else 2]
                for a, b in pads:
                    last = nc.gpsimd.memset(z[:, :, a:b], 0.0)
                last.then_inc(zpad, 1)
                pool.wait_ge(zpad, layer + 1)
                cw = CVW if layer == 0 else N
                for k in POOL_TILES:
                    pool.wait_ge(slot_free[0], USES[layer, "u"] + k + 1)
                    acc = cv[:, k, 0:cw]
                    chain.link(nc.gpsimd.tensor_scalar(acc, z[:, k, 0:cw], col("w_dw", k, layer),
                                                       col("b_dw", k, layer), ALU.mult, ALU.add))
                    for tap in range(1, TAPS):
                        chain.link(nc.gpsimd.tensor_scalar(scratch[:, 0:cw], z[:, k, tap:tap + cw],
                                                           col("w_dw", tap * CT + k, layer), 0.0, ALU.mult, ALU.add))
                        last = nc.gpsimd.tensor_tensor(acc, acc, scratch[:, 0:cw], ALU.add)
                        if tap < TAPS - 1:
                            chain.link(last)
                    last.then_inc(conv_ok, 1)


def ktiles_after(layer, name, i):
    p = FIRST[layer, name] + (i if isinstance(i, int) else 0) + 1
    return KTILES[min(p, PAIRS - 1)] if isinstance(i, int) else KTILES[FIRST[layer, name]]


def weight_blocks(w, outs, k_tiles):
    blocks = np.stack([np.concatenate([w[:, P * k:P * k + P, o:o + P] for k in ks], axis=2)
                       for o, ks in zip(outs, k_tiles)], axis=1)
    layers, n = blocks.shape[:2]
    return np.ascontiguousarray(blocks.reshape(layers, n // 2, 2, P, -1).transpose(0, 2, 1, 3, 4))


def host_constants():
    tok = np.arange(N)
    freqs = (np.float32(10000.0) ** (-np.arange(FREQS, dtype=np.float32) / np.float32(FREQS))).astype(np.float32)
    ang = np.zeros((HD, N), np.float32)
    for d in range(HD):
        pos = (tok // GRID_W if d < HD // 2 else tok % GRID_W).astype(np.float32)
        ang[d] = pos * freqs[d % FREQS]
    ang = np.concatenate([ang, ang]).astype(np.float64)
    sign = np.where(np.arange(P) % (2 * FREQS) < FREQS, -1.0, 1.0)[:, None]
    rope = np.stack([np.cos(ang), sign * np.sin(ang)]).astype(np.float32)
    q, k = np.arange(P)[:, None], np.arange(P)[None, :]
    masks = np.concatenate([np.where(k >= q, 0.0, MASKED), np.where(k <= q, 0.0, MASKED)], axis=1).astype(np.float32)
    return rope, np.eye(P, dtype=np.float32), masks


def kernel(**inputs):
    import concourse.bacc as bacc
    from concourse.bass_utils import run_bass_kernel_spmd

    a = {k: np.asarray(v) for k, v in inputs.items()}

    def cols(v):
        return v.reshape(-1, P).T

    table = []
    for l in range(DEPTH):
        table += [cols(a[n][l]) for n in ("b_ada", "g_mix", "g_ffn", "g_attn_out", "g_conv_out", "b_dw", "ln_g", "ln_b", "w_dw")]
        table.append(np.broadcast_to(a["attn_sink"][l][None, :], (P, HEADS)))
    table.append(cols(a["g_final"]))
    table.append(np.stack([cols(a["c"][0]), cols(a["c_ctx"])], axis=2).reshape(P, 2 * DT))
    tokens = np.concatenate([a["x"][0], a["ctx"][0]], axis=0)

    q_k_v, half = AW + 2 * KV * HD, AW + 2 * KV * HD + CW
    mix = [o for i in range(CT) for o in (q_k_v + P * i, half + P * i)] + [P * i for i in range(q_k_v // P)]
    w_mix = weight_blocks(a["w_in"], mix, [range(DT)] * len(mix))
    wo = a["w_out"].reshape(DEPTH, 2, CT, P, DT // 2, 2, P)
    wo = wo.transpose(0, 1, 4, 3, 5, 2, 6).reshape(DEPTH, 2, 2, 2, P, 2 * CT * P)
    w_out = np.ascontiguousarray(wo.transpose(0, 3, 1, 2, 4, 5).reshape(DEPTH, 2, 4, P, 2 * CT * P))
    gu = [o for i in range(FT) for o in (P * i, D_FF + P * i)]
    w_gu = weight_blocks(a["w_gate_up"], gu, [range(DT)] * len(gu))
    dn = [weight_blocks(a["w_down"], [P * i for i in range(DT)],
                        [range(sum(CHUNKS[:c]), sum(CHUNKS[:c + 1]))] * DT) for c in range(3)]
    w_ada = np.ascontiguousarray(a["w_ada"].reshape(DEPTH, DT, P, AG, AGW).transpose(0, 3, 1, 2, 4)
                                 .reshape(DEPTH * AG, DT, P, AGW))
    rope, ident, masks = host_constants()
    arrays = {
        "xT": np.ascontiguousarray(tokens.T.reshape(DT, P, T)), "params": np.ascontiguousarray(np.concatenate(table, axis=1)),
        "w_ada": w_ada, "w_mix": w_mix, "w_out": w_out, "w_gu": w_gu, "w_dn0": dn[0], "w_dn1": dn[1], "w_dn2": dn[2],
        "rope": rope, "ident_in": ident, "masks_in": masks,
    }
    nc = bacc.Bacc("TRN2", target_bir_lowering=False, num_devices=1)
    args = {n: nc.dram_tensor(f"in_{n}", v.shape, mybir.dt.from_np(v.dtype), kind="ExternalInput").ap()
            for n, v in arrays.items()}
    out = nc.dram_tensor("out_yT", (DT, P, N), F32, kind="ExternalOutput").ap()
    hybrid_backbone(nc, *args.values(), out)
    r = run_bass_kernel_spmd(nc, [{f"in_{n}": v for n, v in arrays.items()}], core_ids=[0])
    y = r.results[0]["out_yT"]
    return np.ascontiguousarray(y.reshape(D, N).T).reshape(1, N, D)
```

```python
import math
from contextlib import ExitStack

import numpy as np

import concourse.bass as bass
from concourse import mybir

F32, F32R, BF16 = mybir.dt.float32, mybir.dt.float32r, mybir.dt.bfloat16
ALU, ACT, AX = mybir.AluOpType, mybir.ActivationFunctionType, mybir.AxisListType

P = 128
D = 1024
DT = D // P
DEPTH = 2
N, L = 512, 256
T = N + L
TB, NB, LB = T // P, N // P, L // P
HEADS, KV, HD = 8, 2, 64
GRP = HEADS // KV
AW = HEADS * HD
CW = D - AW
CT = CW // P
TAPS = 31
PAD = TAPS // 2
HC = N + 2
HW = HC + L + 2
D_FF = 2816
FT = D_FF // P
CHUNKS = (8, 8, 6)
GRID_W, FREQS = 64, HD // 4
EPS = 1e-6
SCALE = HD ** -0.5
MASKED = -1e30
MODS = 6
AG = 3
AGW = MODS * D // AG
ZW = PAD + N + 2 * PAD + L + PAD
CC = N + 2 * PAD
CVW = CC + L

OFF, n_ = {}, 0
for name_, width_ in (("b_ada", MODS * DT), ("g_mix", DT), ("g_ffn", DT), ("g_attn", CT), ("g_conv", CT),
                      ("b_dw", CT), ("ln_g", CT), ("ln_b", CT), ("w_dw", TAPS * CT), ("sink", HEADS)):
    OFF[name_] = n_
    n_ += width_
LAYER_COLS = n_
OFF["g_final"], OFF["cond"] = DEPTH * LAYER_COLS, DEPTH * LAYER_COLS + DT
COLS = DEPTH * LAYER_COLS + DT + 2 * DT

PHASES = [("u", 4, 8), ("qkv", 3, 8), ("oa", 2, 8), ("ob", 2, 8)]
for c_, k_ in enumerate(CHUNKS):
    PHASES += [(f"gu{c_}", k_, 8), (f"dn{c_}", 4, k_)]
PAIRS_OF = {name_: pairs_ for name_, pairs_, _ in PHASES}
FIRST, USES = {}, {}
n_ = m_ = 0
for l_ in range(DEPTH):
    for name_, pairs_, _k in PHASES:
        FIRST[l_, name_], USES[l_, name_] = n_, m_
        n_ += pairs_
        m_ += 4 if name_ in ("oa", "ob") else pairs_
PAIRS = n_
KTILES = [k for _l in range(DEPTH) for _n, pairs, k in PHASES for _p in range(pairs)]


def queries(layer):
    out = []
    for b in range(TB if layer == 0 else NB):
        keys = [NB, NB + 1] + ([t for t in (b - 1, b, b + 1) if 0 <= t < NB] if b < NB else [])
        out += [(g, b, keys) for g in range(KV)]
    return out


class Chain:

    def __init__(self, engine, sem):
        self.engine, self.sem, self.n = engine, sem, 0

    def link(self, instruction):
        instruction.then_inc(self.sem, 1)
        self.n += 1
        self.engine.wait_ge(self.sem, self.n)


def hybrid_backbone(nc, xT, params, w_ada, w_mix, w_out, w_gu, w_dn0, w_dn1, w_dn2,
                    rope, ident_in, masks_in, out):
    with ExitStack() as ctx:
        def sb(name, shape, dt=F32):
            return ctx.enter_context(nc.sbuf_tensor(name, shape, dt))

        def sem(name):
            return ctx.enter_context(nc.semaphore(name))

        x = sb("x", [P, DT, T])
        raw = [sb(f"raw{j}", [P, DT, P]) for j in range(2)]
        wH = [sb(f"w_high{j}", [P, DT, P], F32R) for j in range(2)]
        wL = [sb(f"w_low{j}", [P, DT, P], F32R) for j in range(2)]
        ada_raw = [sb(f"ada_raw{j}", [P, AGW]) for j in range(2)]
        ssum = sb("ssum", [P, CVW])
        sq = [sb(f"sq{j}", [P, T]) for j in range(2)]
        tmp = [sb(f"tmp{j}", [P, T]) for j in range(2)]
        act_out = sb("act_out", [P, T])
        ada_row = act_out[:, 0:AGW // 4]
        rs = sb("inv_root", [P, T])
        shifted = sb("shift_product", [P, 2, 2])
        shifted_rot = sb("shift_product_rotated", [P, 2])
        scratch = sb("diag_or_product", [P, CVW])
        diag = scratch[:, 0:T].rearrange("p (b t) -> p b t", t=P)
        par = sb("par", [P, COLS])
        mod = sb("mod", [P, DEPTH, MODS * DT, 2])
        gain = sb("gain", [P, DEPTH, 2, DT, 2])
        cond = sb("cond", [P, DT, 32])
        cosT = sb("cosT", [P, N])
        sinT = sb("sinT", [P, N])
        ident = sb("ident", [P, P])
        identb = sb("identb", [P, P], BF16)
        maskb = sb("maskb", [P, 2, P], BF16)
        mean_col = sb("mean_col", [P, 2])
        ones = sb("ones", [P, P])
        per_tok = sb("per_tok", [P, 2, TB])
        mx = sb("row_max", [P, 4])
        nmax = sb("neg_max", [P, 4])
        nsink = sb("nsink", [P, DEPTH, HEADS])
        esink = sb("esink", [P, 4])
        psums = sb("psums", [P, 4])
        eps = sb("eps", [P, 1])

        with ExitStack() as h_scope:
            hH = h_scope.enter_context(nc.sbuf_tensor("h_high", [P, DT, HW], F32R))
            hL = h_scope.enter_context(nc.sbuf_tensor("h_low", [P, DT, HW], F32R))
            with ExitStack() as s:
                z = s.enter_context(nc.sbuf_tensor("z_padded", [P, CT, ZW], F32))
                cv = s.enter_context(nc.sbuf_tensor("conv", [P, CT, CVW], F32))
                Q2 = s.enter_context(nc.sbuf_tensor("q_stacked", [P, HEADS, T], F32R))
                K2 = s.enter_context(nc.sbuf_tensor("k_stacked", [P, KV, 2, T], F32R))
            with ExitStack() as s:
                aH = s.enter_context(nc.sbuf_tensor("ff_high", [P, max(CHUNKS), T], F32R))
                aL = s.enter_context(nc.sbuf_tensor("ff_low", [P, max(CHUNKS), T], F32R))
        with ExitStack() as s:
            prob = s.enter_context(nc.sbuf_tensor("prob", [P, 2, 5 * P], F32))
            V2 = s.enter_context(nc.sbuf_tensor("v_stacked", [P, TB, KV, 2, HD], F32R))
            s.enter_context(nc.sbuf_tensor("gap", [P, CT * HW - 5 * P * 2 - TB * KV * 2 * HD], F32))
            aT = s.enter_context(nc.sbuf_tensor("attn_out", [P, CT, T], F32))
            s.enter_context(nc.sbuf_tensor("gap2", [P, CT * (HW - T)], F32))
            PT = s.enter_context(nc.sbuf_tensor("probT", [P, 2, 5, GRP, P], F32R))

        bank = ctx.enter_context(nc.psum_tensor("banks", [P, 8, 512], F32))
        wide = bank[:].rearrange("p b n -> p (b n)")
        ADA, SMALL, BC, PTB = 4, 5, 6, 4
        probs = [prob[:, 0, :], prob[:, 1, :], sq[1][:, 0:5 * P]]

        par_in, x_in, const_in, mask_in = sem("par_in"), sem("x_in"), sem("const_in"), sem("mask_in")
        raw_in = [sem(f"raw_in{j}") for j in range(2)]
        ada_in = [sem(f"ada_in{j}") for j in range(2)]
        y_out = sem("out_stored")
        w_high, w_low = sem("w_high_ready"), sem("w_low_ready")
        gemm = sem("gemm_tile_done")
        slot_free = [sem(f"slot_read_out{j}") for j in range(2)]
        consts, cond_ok, casts_ok, nsink_ok = sem("constants_set"), sem("cond_ready"), sem("casts_ready"), sem("neg_sink_ready")
        ada_mm, ada_rowed = sem("ada_unit_done"), sem("ada_rows_copied")
        ada_tr, ada_cols = sem("ada_rows_transposed"), sem("ada_columns_ready")
        sum_ok, tok_mm, tok_root = sem("feature_sum_ready"), sem("token_mean_done"), sem("token_root_done")
        diag_ok, bc_ok = sem("diagonal_ready"), sem("stat_broadcast_done")
        sq_ok, sq_used = sem("square_ready"), sem("square_added")
        high_ok, h_ok, rs_ok = sem("h_high_ready"), sem("h_tile_ready"), sem("inv_root_ready")
        sh_high, sh_ok, sh_out = sem("shift_high_ready"), sem("shift_ready"), sem("gated_tile_ready")
        x_added, gate_ok, z_ok, ff_ok = sem("x_tile_added"), sem("gate_ready"), sem("z_ready"), sem("ff_product_ready")
        conv_ok, zpad, shared_ok = sem("conv_tile_done"), sem("z_padding_zero"), sem("shared_taps_summed")
        r_ok, qk_high, qk_ok = sem("rope_done"), sem("qk_high_ready"), sem("qk_ready")
        v_ok, v_tr, v_high, v_ready = sem("v_copied"), sem("v_transposed"), sem("v_high_ready"), sem("v_ready")
        s_ok, max_ok, exp_ok, prob_ok = sem("scores_done"), sem("max_ready"), sem("exp_ready"), sem("prob_ready")
        row_ok, sink_ok, recip_ok = sem("row_max_ready"), sem("sink_added"), sem("inv_sum_ready")
        pt_ps, pt_high, pt_ok = sem("prob_transposed"), sem("probT_high_ready"), sem("probT_ready")
        pv_ok, pv_low, a_ok = sem("pv_done"), sem("pv_low_copied"), sem("attn_group_ready")
        ln_d, ln_y, ln_s = sem("conv_centred"), sem("conv_scaled"), sem("conv_silu_done")
        ff_high, ff_low = sem("ff_high_ready"), sem("ff_low_ready")
        y_ok = sem("out_tile_ready")
        dve_self, pool_self = sem("dve_self"), sem("pool_self")

        def col(name, i, layer=0):
            o = (layer * LAYER_COLS if name not in ("g_final", "cond") else 0) + OFF[name] + i
            return par[:, o:o + 1]

        def streams(context):
            return [(0, N, 0)] + ([(N, T, 1)] if context else [])

        def hcols(a, b):
            return slice(a, b) if a < N else slice(a + HC - N, b + HC - N)

        def mod_cols(context):
            return [(0, 0, N), (1, HC, HW)] if context else [(0, 0, N // 2), (1, N // 2, HC)]

        def tok_cols(context, of_h):
            return [(0, 0, N)] + ([(1, *((HC, HC + L) if of_h else (N, T)))] if context else [])

        def product(slot, context):
            if context:
                return wide[:, 1024 * slot:1024 * slot + T], lambda ap: ap[:, 0:T]
            return bank[:, 2 * slot:2 * slot + 2, 0:N // 2], lambda ap: ap[:, 0:N].rearrange("p (h n) -> p h n", h=2)

        def gains(layer, which, context, k):
            return [(a, b, gain[:, layer, which, k, v:v + 1]) for a, b, v in streams(context)]

        def shift_cols(slot):
            return bank[:, 2 * slot + 1, L:L + 2]

        STATS = [(l, s) for l in range(DEPTH) for s in ("n1", "an", "mean", "var", "cn", "n2")] + [(DEPTH, "n1")]
        stat_index = {s: i for i, s in enumerate(STATS)}
        root_index = {s: i for i, s in enumerate([s for s in STATS if s[1] != "mean"])}
        rs_index = {s: i for i, s in enumerate([s for s in STATS if s[1] not in ("mean", "var")])}
        h_index, n = {}, 0
        for s in STATS[:-1]:
            if s[1] in ("n1", "an", "cn", "n2"):
                h_index[s] = n
                n += CT if s[1] in ("an", "cn") else DT
        sq_index, n = {}, 0
        for l in range(DEPTH):
            for s, tiles in [("x", DT)] * (l == 0) + [("an", CT), ("var", CT), ("cn", CT), ("ob", DT), ("dn2", DT)]:
                sq_index[l, s] = n
                n += tiles
        groups = [(l, q) for l in range(DEPTH) for q in range(len(queries(l)))]
        group_index = {g: i for i, g in enumerate(groups)}
        ADA_IN = {(0, "u"): 1, (0, "qkv"): 2, (0, "dn0"): 3, (0, "dn1"): 4, (0, "dn2"): 5}
        TURN_IN = {(0, "qkv"): 1, (0, "gu1"): 3, (0, "gu2"): 4, (1, "u"): 5}

        def gates_before(layer, where):
            return layer * (CT + FT) + (CT if where == "gu" else 0)

        def ada_units(layer, name, block):
            if (layer, name) not in ADA_IN:
                return []
            blocks = 2 * PAIRS_OF[name]
            return [(ADA_IN[layer, name], k) for k in range(DT) if k * (blocks - 1) // (DT - 1) == block]

        POOL_TILES = (0, 2, 3)
        SHARED = 10
        DVE_TAPS = [(0, tap) for tap in range(SHARED)] + [(k, tap) for k in range(CT) if k not in POOL_TILES
                                                         for tap in range(TAPS)]
        CONV_IN_U = (((0, 0), (5, 8), (5, 5), (5, 4)), ((0, 0), (5, 8), (5, 5), (5, 4)))
        CONV_IN_QKV = ((2, 2, 2, 2, 0, TAPS), (2, 2, 2, 2, 0, TAPS))
        STAT_AFTER = {"oa": {0: [(3, "an", 0)], 1: [(1, "an", 1)], 2: [(0, "mean", 1)], 3: [(3, "var", 0)],
                             4: [(2, "var", 1)]},
                      "ob": {1: [(3, "cn", 0), (3, "cn", 1)]}}

        block = ctx.enter_context(nc.Block())

        @block.sync
        def _(sp):
            sp.dma_start(par[:], params).then_inc(par_in, 16)

            def load_ada(unit):
                i = unit[0] * DT + unit[1]
                if i >= 2:
                    sp.wait_ge(ada_mm, i - 1)
                sp.dma_start(ada_raw[i % 2][:], w_ada[unit[0], unit[1]]).then_inc(ada_in[i % 2], 16)

            for k in range(2):
                load_ada((0, k))
            for k in range(DT):
                sp.dma_start(x[:, k, :], xT[k]).then_inc(x_in, 16)
                if k % 2 and k < 5:
                    load_ada((0, k // 2 + 2))
                if k == 3:
                    sp.dma_start(ident[:], ident_in).then_inc(const_in, 16)
                    sp.dma_start(act_out[:, 0:2 * P], masks_in).then_inc(mask_in, 16)
            for k in range(4, DT):
                load_ada((0, k))
                if k >= DT - 2:
                    sp.dma_start(raw[k % 2][:].rearrange("p k m -> p (k m)"), w_mix[0, k % 2, 0]).then_inc(raw_in[k % 2], 16)
            sp.dma_start(cosT[:], rope[0]).then_inc(const_in, 16)
            sp.dma_start(sinT[:], rope[1]).then_inc(const_in, 16)
            for layer in range(DEPTH):
                for name, pairs, ktiles in PHASES:
                    base = FIRST[layer, name]
                    src, skip = {"u": (w_mix, 0), "qkv": (w_mix, 4), "oa": (w_out, 0), "ob": (w_out, 2),
                                 "gu0": (w_gu, 0), "gu1": (w_gu, CHUNKS[0]), "gu2": (w_gu, CHUNKS[0] + CHUNKS[1]),
                                 "dn0": (w_dn0, 0), "dn1": (w_dn1, 0), "dn2": (w_dn2, 0)}[name]

                    def load_block(i, j):
                        sp.dma_start(raw[j][:, 0:ktiles, :],
                                     src[layer, j, i + skip].rearrange("p (k m) -> p k m", m=P)).then_inc(raw_in[j], 16)

                    if (layer, name) in ADA_IN:
                        for i in range(pairs):
                            for j in range(2):
                                if base + i > 0:
                                    sp.wait_ge(w_low, 2 * (base + i) + j - 1)
                                    load_block(i, j)
                                for u in ada_units(layer, name, 2 * i + j):
                                    load_ada(u)
                    else:
                        with sp.Fori(0, pairs) as i:
                            for j in range(2):
                                sp.wait_ge(w_low, i * 2 + (2 * base + j - 1))
                                load_block(i, j)
            for k in range(DT):
                sp.wait_ge(y_ok, k + 1)
                sp.dma_start(out[k], x[:, k, 0:N]).then_inc(y_out, 16)
            sp.wait_ge(y_out, 16 * DT)

        @block.tensor
        def _(pe):
            mm = nc.tensor.matmul

            def ada_unit(unit):
                g, k = unit
                i = g * DT + k
                pe.wait_ge(ada_in[i % 2], 16 * (i // 2 + 1))
                for q in range(4):
                    last = mm(bank[32 * q:32 * q + 32, ADA, :], cond[:, k, :], ada_raw[i % 2][:, 512 * q:512 * q + 512],
                              start=(k == 0), stop=(k == DT - 1), tile_position=(0, 32 * q))
                last.then_inc(ada_mm, 1)

            def ada_turn(g):
                pe.wait_ge(ada_rowed, g + 1)
                for j in range(4):
                    last = nc.tensor.transpose(bank[:, SMALL, P * j:P * j + P], ada_row[:, P * j:P * j + P], ident[:])
                last.then_inc(ada_tr, 1)

            def stat_tokens(key, blocks):
                pe.wait_ge(sum_ok, stat_index[key] + 1)
                width = mean_col[:, 0:1] if key[1] in ("n1", "n2") else mean_col[:, 1:2]
                for b in range(blocks):
                    last = mm(bank[:, SMALL, b:b + 1], ssum[:, P * b:P * b + P], width, start=True, stop=True)
                last.then_inc(tok_mm, 1)

            def stat_broadcast(key, blocks):
                if key[1] == "mean":
                    pe.wait_ge(sum_ok, stat_index[key] + 1)
                    pe.wait_ge(rs_ok, rs_index[key[0], "an"] + 1)
                    lat, con = ssum[:, 0:N], ssum[:, CC:CC + L]
                else:
                    pe.wait_ge(diag_ok, root_index[key] + 1)
                    lat, con = scratch[:, 0:N], scratch[:, N:T]
                last = mm(bank[:, BC, 0:N], ones[:], lat, start=True, stop=True)
                if blocks > NB:
                    last = mm(bank[:, BC + 1, 0:L], ones[:], con, start=True, stop=True)
                last.then_inc(bc_ok, 1)

            def tile_product(w, k0_w, slot, ktiles, rhsH, rhsL, k0_rhs, cols, ready=None, after=()):
                for k in range(ktiles):
                    if ready is not None:
                        pe.wait_ge(ready[0], ready[1] + k + 1)
                    for n, (weights, rhs) in enumerate(((wH, rhsH), (wH, rhsL), (wL, rhsH))):
                        for bk, a, b in cols:
                            last = mm(bank[:, 2 * slot + bk, 0:b - a], weights[w][:, k0_w + k, :],
                                      rhs[:, k0_rhs + k, a:b], start=(k == 0 and n == 0),
                                      stop=(k == ktiles - 1 and n == 2))
                    if k == ktiles - 1:
                        last.then_inc(gemm, 1)
                    for at, issue in after:
                        if at == k:
                            issue()

            def gemm_block(layer, name, i, j, ktiles, rhsH, rhsL, cols, ready=None, after=()):
                pe.wait_ge(w_low, i * 2 + (2 * FIRST[layer, name] + j + 1))
                if not isinstance(i, int) or USES[layer, name] + i > 0:
                    pe.wait_ge(slot_free[j], i + USES[layer, name])
                tile_product(j, 0, j, ktiles, rhsH, rhsL, 0, cols, ready, after)

            def phase(layer, name, ktiles, rhsH, rhsL, cols, ready=None, key=None, blocks=TB):
                pairs = PAIRS_OF[name]
                with_ada = (layer, name) in ADA_IN
                after = {0: [], 1: []}
                if key is not None:
                    after[0].append((5 if blocks == TB else 7, lambda: stat_tokens(key, blocks)))
                    after[1].append((0 if blocks == TB else 2, lambda: stat_broadcast(key, blocks)))
                if (layer, name) in TURN_IN:
                    after[name == "u"].append((3, lambda: ada_turn(TURN_IN[layer, name])))
                for i in range(pairs if with_ada else 1):
                    for j in range(2):
                        gemm_block(layer, name, i, j, ktiles, rhsH, rhsL, cols, ready if i + j == 0 else None,
                                   after[j] if i == 0 else ())
                        for u in ada_units(layer, name, 2 * i + j):
                            ada_unit(u)
                if not with_ada:
                    with pe.Fori(1, pairs) as i:
                        for j in range(2):
                            gemm_block(layer, name, i, j, ktiles, rhsH, rhsL, cols)

            def out_phase(layer, name, half, blocks):
                for t in range(DT):
                    i, j, m = t // 4, t // 2 % 2, t % 2
                    if m == 0:
                        pe.wait_ge(w_low, 2 * (FIRST[layer, name] + i) + j + 1)
                    if t >= 2 or half:
                        pe.wait_ge(slot_free[m], USES[layer, name] + t // 2)
                    stats = [(k, lambda which=which, part=part:
                              (stat_broadcast if part else stat_tokens)((layer, which), blocks))
                             for k, which, part in STAT_AFTER[name].get(t, ())]
                    tile_product(j, 4 * m, m, CT, hH, hL, CT * half, tok_cols(blocks == TB, True),
                                 (h_ok, h_index[layer, "cn" if half else "an"]) if t == 0 else None, stats)

            def attention(layer):
                qs = queries(layer)
                order = [(q, i) for q in range(len(qs)) for i in range(GRP)]
                unit0 = GRP * group_index[layer, 0]

                def scores(n):
                    q, i = order[n]
                    g, b, keys = qs[q]
                    u = unit0 + n
                    if n == 0:
                        pe.wait_ge(qk_ok, 5 * (layer + 1))
                        for j in range(2):
                            pe.wait_ge(slot_free[j], USES[layer, "oa"])
                    if u >= 2:
                        pe.wait_ge(exp_ok, u - 1)
                    s = 1024 * (u % 2)
                    window = keys[2:]
                    spans = [(0, N, 2 * P)]
                    if window:
                        spans.append((2 * P, P * window[0], P * min(2, len(window))))
                    if len(window) == 3:
                        spans.append((4 * P, P * window[2], P))
                    parts = [(at, w, Q2[:, g * GRP + i, P * b:P * b + P], K2[:, g, part, tok:tok + w])
                             for at, tok, w in spans for part in range(2)]
                    parts += [((2 + m) * P, P, identb[:], maskb[:, 0 if t < b else 1, :])
                              for m, t in enumerate(window) if t != b]
                    in_bank = [at // 512 for at, *_ in parts]
                    for m, (at, w, lhs, rhs) in enumerate(parts):
                        last = mm(wide[:, s + at:s + at + w], lhs, rhs, start=in_bank[m] not in in_bank[:m],
                                  stop=in_bank[m] not in in_bank[m + 1:], skip_group_check=True)
                    last.then_inc(s_ok, 1)

                def turn(n):
                    u, keys = unit0 + n, qs[order[n][0]][2]
                    pe.wait_ge(prob_ok, u + 1)
                    if n:
                        pe.wait_ge(pt_ok, u)
                    else:
                        pe.wait_ge(v_ready, layer + 1)
                    for m in range(len(keys)):
                        last = nc.tensor.transpose(wide[:, 512 * PTB + P * m:512 * PTB + P * m + P],
                                                   probs[u % 3][:, P * m:P * m + P], ident[:])
                    last.then_inc(pt_ps, 1)

                def values(n):
                    q, i = order[n]
                    g, b, keys = qs[q]
                    h2 = (unit0 + n) // 2
                    pe.wait_ge(pt_ok, 2 * h2 + 2)
                    if h2 >= 2:
                        pe.wait_ge(a_ok, h2 - 1)
                    for m, t in enumerate(keys):
                        for part in range(2):
                            last = mm(bank[:, BC + h2 % 2, 0:2 * P], V2[:, t, g, :, :].rearrange("p a d -> p (a d)"),
                                      PT[:, part, m, i - 1:i + 1, :].rearrange("p h q -> p (h q)"),
                                      start=(m == 0 and part == 0), stop=(m == len(keys) - 1 and part == 1))
                    last.then_inc(pv_ok, 1)

                scores(0)
                pe.wait_ge(v_ok, layer + 1)
                pe.wait_ge(ada_cols, AG * (layer + 1))
                for b in range(TB):
                    last = nc.tensor.transpose(wide[:, 512 * PTB + P * b:512 * PTB + P * b + P],
                                               tmp[1][:, P * b:P * b + P], ident[:])
                last.then_inc(v_tr, 1)
                for n in range(1, 4):
                    scores(n)
                for n in range(len(order)):
                    turn(n)
                    if n + 4 < len(order):
                        scores(n + 4)
                    if n and n % 2 == 0:
                        values(n - 1)
                values(len(order) - 1)

            pe.wait_ge(consts, 4)
            pe.wait_ge(cond_ok, 1)
            for k in range(DT - 1):
                ada_unit((0, k))
            stat_tokens((0, "n1"), TB)
            ada_unit((0, DT - 1))
            pe.wait_ge(const_in, 48)
            stat_broadcast((0, "n1"), TB)
            ada_turn(0)
            for layer in range(DEPTH):
                context = layer == 0
                blocks = TB if context else NB
                pe.wait_ge(sh_ok, 2 * layer + 1)
                phase(layer, "u", DT, hH, hL, mod_cols(context), (h_ok, h_index[layer, "n1"]),
                      (layer, "n1") if layer else None, TB)
                for i in range(PAIRS_OF["qkv"]):
                    for j in range(2):
                        turn = i + j == 0 and (layer, "qkv") in TURN_IN
                        keys_or_values = 2 * i + j in (0, 5)
                        gemm_block(layer, "qkv", i, j, DT, hH, hL, mod_cols(context or keys_or_values),
                                   after=[(DT - 1, lambda: ada_turn(TURN_IN[layer, "qkv"]))] if turn else ())
                        for u in ada_units(layer, "qkv", 2 * i + j):
                            ada_unit(u)
                if (layer, "qkv") in ADA_IN:
                    ada_turn(ADA_IN[layer, "qkv"])
                attention(layer)
                out_phase(layer, "oa", 0, blocks)
                out_phase(layer, "ob", 1, blocks)
                pe.wait_ge(sh_ok, 2 * layer + 2)
                for c, tiles in enumerate(CHUNKS):
                    phase(layer, f"gu{c}", DT, hH, hL, mod_cols(context), (h_ok, h_index[layer, "n2"]) if c == 0 else None,
                          (layer, "n2") if c == 0 else None, blocks)
                    phase(layer, f"dn{c}", tiles, aH, aL, tok_cols(context, False), (ff_low, layer * FT + sum(CHUNKS[:c])))
            stat_tokens((DEPTH, "n1"), NB)
            stat_broadcast((DEPTH, "n1"), NB)

        @block.scalar
        def _(act):
            f = nc.scalar.activation

            def split_high(layer, name, i, j):
                step = 4 if name in ("oa", "ob") else 2
                done = 2 * USES[layer, name] + (2 * j + 2 if step == 4 else j + 1)
                act.wait_ge(gemm, i * step + done)
                act.wait_ge(raw_in[j], i * 16 + 16 * (FIRST[layer, name] + 2))
                k = ktiles_after(layer, name, i)
                f(wH[j][:, 0:k, :], raw[j][:, 0:k, :], ACT.Copy).then_inc(w_high, 1)

            def first_high():
                for j in range(2):
                    act.wait_ge(raw_in[j], 16)
                    f(wH[j][:], raw[j][:], ACT.Copy).then_inc(w_high, 1)

            def square(series, layer, k, src):
                n = sq_index[layer, series] + k
                if n >= 2:
                    act.wait_ge(sq_used, n - 1)
                w = src.shape[-1]
                f(sq[n % 2][:, 0:w], src, ACT.Square).then_inc(sq_ok, 1)

            def root(key, blocks):
                act.wait_ge(tok_mm, root_index[key] + 1)
                f(per_tok[:, 0, 0:blocks], bank[:, SMALL, 0:blocks], ACT.Sqrt, bias=eps[:]).then_inc(tok_root, 1)

            def copy_root(key, width):
                act.wait_ge(bc_ok, stat_index[key] + 1)
                f(rs[:, 0:width], wide[:, 512 * BC:512 * BC + width], ACT.Copy).then_inc(rs_ok, 1)

            def high(k, src, scales):
                for a, b, scale in scales:
                    last = f(hH[:, k, hcols(a, b)], src[:, a:b], ACT.Copy, scale=scale)
                last.then_inc(high_ok, 1)

            def shift_high(layer, shift):
                for at in (N, HW - 2):
                    last = f(hH[:, :, at:at + 2], mod[:, layer, shift * DT:(shift + 1) * DT, :], ACT.Copy)
                last.then_inc(sh_high, 1)

            def ada_rows(g):
                act.wait_ge(ada_mm, DT * (g + 1))
                if g == 1:
                    act.wait_ge(z_ok, CT)
                f(ada_row, bank[:, ADA, :], ACT.Copy).then_inc(ada_rowed, 1)

            def ada_after(layer, name):
                if (layer, name) in ADA_IN:
                    ada_rows(ADA_IN[layer, name])

            def attention(layer):
                qs = queries(layer)
                order = [(q, i) for q in range(len(qs)) for i in range(GRP)]
                unit0 = GRP * group_index[layer, 0]

                def pv_copy(h2):
                    act.wait_ge(pv_ok, h2 + 1)
                    if h2 >= 2:
                        act.wait_ge(a_ok, h2 - 1)
                    f(act_out[0:HD, 2 * P * (h2 % 2):2 * P * (h2 % 2) + 2 * P], bank[HD:P, BC + h2 % 2, 0:2 * P],
                      ACT.Copy).then_inc(pv_low, 1)

                def exponential(n):
                    u, (q, i) = unit0 + n, order[n]
                    w, c = P * len(qs[q][2]), u % 4
                    act.wait_ge(max_ok, u + 1)
                    if u >= 3:
                        act.wait_ge(pt_ps, u - 2)
                    f(probs[u % 3][:, 0:w], wide[:, 1024 * (u % 2):1024 * (u % 2) + w], ACT.Exp,
                      bias=nmax[:, c:c + 1], scale=SCALE, accum_out=psums[:, c:c + 1])
                    f(esink[:, c:c + 1], col("sink", qs[q][0] * GRP + i, layer), ACT.Exp,
                      bias=nmax[:, c:c + 1]).then_inc(exp_ok, 1)

                def divide(n):
                    u, w = unit0 + n, P * len(qs[order[n][0]][2])
                    act.wait_ge(recip_ok, u + 1)
                    f(probs[u % 3][:, 0:w], probs[u % 3][:, 0:w], ACT.Copy, scale=psums[:, u % 4:u % 4 + 1])\
                        .then_inc(prob_ok, 1)

                def prob_high(n):
                    u, (q, i) = unit0 + n, order[n]
                    if n >= GRP:
                        act.wait_ge(pv_ok, (u - GRP) // 2 + 1)
                    w = len(qs[q][2])
                    act.wait_ge(pt_ps, u + 1)
                    f(PT[:, 0, 0:w, i, :], wide[:, 512 * PTB:512 * PTB + P * w].rearrange("p (k q) -> p k q", k=w),
                      ACT.Copy).then_inc(pt_high, 1)

                act.wait_ge(v_tr, layer + 1)
                f(V2[:, :, :, 0, :], wide[:, 512 * PTB:512 * PTB + T].rearrange("p (t g d) -> p t g d", t=TB, g=KV),
                  ACT.Copy).then_inc(v_high, 1)
                for n in range(-3, len(order)):
                    if n >= 0:
                        prob_high(n)
                    if n + 3 < len(order):
                        exponential(n + 3)
                    if 0 <= n + 2 < len(order):
                        divide(n + 2)
                    if n % 2 == 1 and n >= 3:
                        pv_copy((unit0 + n) // 2 - 1)
                pv_copy((unit0 + len(order)) // 2 - 1)

            act.wait_ge(par_in, 16)
            act.wait_ge(consts, 4)
            f(cond[:, :, 0:2], par[:, OFF["cond"]:OFF["cond"] + 2 * DT].rearrange("p (k v) -> p k v", v=2),
              ACT.Silu).then_inc(cond_ok, 1)
            act.wait_ge(x_in, 16 * DT)
            for k in range(DT):
                square("x", 0, k, x[:, k, :])
            act.wait_ge(const_in, 48)
            f(identb[:], ident[:], ACT.Copy)
            act.wait_ge(mask_in, 16)
            f(maskb[:].rearrange("p m t -> p (m t)"), act_out[:, 0:2 * P], ACT.Copy).then_inc(casts_ok, 1)
            act.wait_ge(casts_ok, 1)
            root((0, "n1"), TB)
            ada_rows(0)
            first_high()
            copy_root((0, "n1"), T)
            act.wait_ge(ada_cols, 1)
            shift_high(0, 0)
            for k in range(DT):
                high(k, x[:, k, :], gains(0, 0, True, k))
            for layer in range(DEPTH):
                context = layer == 0
                width, blocks = (T, TB) if context else (N, NB)
                if layer:
                    root((layer, "n1"), TB)
                    copy_root((layer, "n1"), T)

                for i in range(PAIRS_OF["u"]):
                    split_high(layer, "u", i, 0)
                    split_high(layer, "u", i, 1)
                    act.wait_ge(slot_free[1], USES[layer, "u"] + i + 1)
                    if CT * layer + i:
                        act.wait_ge(z_ok, CT * layer + i)
                    for a, b, v in streams(context):
                        last = f(act_out[:, a:b], tmp[1][:, a:b], ACT.Sigmoid, bias=shifted[:, 1, v:v + 1])
                    last.then_inc(gate_ok, 1)
                ada_after(layer, "u")

                for i in range(3):
                    for j in range(2):
                        split_high(layer, "qkv", i, j)
                        t = 2 * i + j
                        if 0 < t < 5:
                            act.wait_ge(r_ok, 5 * layer + t + 1)
                            f(Q2[0:HD, 2 * t - 2, 0:width], tmp[j][0:HD, 0:width], ACT.Copy)
                            f(Q2[HD:P, 2 * t - 1, 0:width], tmp[j][HD:P, 0:width], ACT.Copy).then_inc(qk_high, 1)
                        elif t == 0:
                            act.wait_ge(r_ok, 5 * layer + t + 1)
                            for g in range(KV):
                                for half in range(2):
                                    last = f(K2[HD * half:HD * half + HD, g, 0, :], tmp[0][HD * g:HD * g + HD, :], ACT.Copy)
                            last.then_inc(qk_high, 1)
                        else:
                            act.wait_ge(slot_free[1], USES[layer, "qkv"] + 3)
                            for a, b, v in streams(True):
                                last = f(tmp[1][:, a:b], tmp[1][:, a:b], ACT.Identity, bias=shifted[:, 1, v:v + 1])
                            last.then_inc(v_ok, 1)
                ada_after(layer, "qkv")
                attention(layer)

                act.wait_ge(a_ok, 2 * group_index[layer, len(queries(layer)) - 1] + 2)
                for k in range(CT):
                    high(k, aT[:, k, :], [(a, b, col("g_attn", k, layer)) for a, b, _ in streams(context)])
                for k in range(CT):
                    square("an", layer, k, aT[:, k, 0:width])
                root((layer, "an"), blocks)
                copy_root((layer, "an"), width)
                for t in range(DT):
                    if t % 2:
                        split_high(layer, "oa", t // 4, t // 2 % 2)
                    if t == 1:
                        for k in range(CT):
                            act.wait_ge(ln_d, CT * layer + k + 1)
                            square("var", layer, k, z[:, k, 0:width])
                    if t == 4:
                        root((layer, "var"), blocks)
                    if t == 5:
                        for k in range(CT):
                            act.wait_ge(ln_y, CT * layer + k + 1)
                            f(cv[:, k, 0:width], z[:, k, 0:width], ACT.Silu, bias=col("ln_b", k, layer)).then_inc(ln_s, 1)
                            act.wait_ge(ln_s, CT * layer + k + 1)
                            high(CT + k, cv[:, k, :], [(a, b, col("g_conv", k, layer)) for a, b, _ in streams(context)])
                            square("cn", layer, k, cv[:, k, 0:width])
                root((layer, "cn"), blocks)
                shift_high(layer, 3)
                act.wait_ge(slot_free[1], USES[layer, "ob"])
                copy_root((layer, "cn"), width)
                for t in range(DT):
                    if t % 2:
                        split_high(layer, "ob", t // 4, t // 2 % 2)
                    if t == DT - 1:
                        act.wait_ge(gemm, 2 * USES[layer, "gu0"])
                        for k in range(CT, t):
                            high(k, x[:, k, :], gains(layer, 1, context, k))
                    act.wait_ge(x_added, 2 * DT * layer + DT + t + 1)
                    if t < CT or t == DT - 1:
                        high(t, x[:, t, :], gains(layer, 1, context, t))
                    square("ob", layer, t, x[:, t, 0:width])
                root((layer, "n2"), blocks)
                act.wait_ge(slot_free[1], USES[layer, "gu0"])
                copy_root((layer, "n2"), width)

                for c, tiles in enumerate(CHUNKS):
                    gu, dn = f"gu{c}", f"dn{c}"
                    ff = layer * FT + sum(CHUNKS[:c])

                    def gu_pair(i):
                        split_high(layer, gu, i, 0)
                        act.wait_ge(slot_free[0], i + (USES[layer, gu] + 1))
                        for a, b, v in streams(context):
                            last = f(act_out[:, a:b], tmp[0][:, a:b], ACT.Silu, bias=shifted[:, 0, v:v + 1])
                        last.then_inc(gate_ok, 1)
                        split_high(layer, gu, i, 1)
                        act.wait_ge(ff_ok, i + (ff + 1))
                        f(aH[:, i, 0:width], tmp[1][:, 0:width], ACT.Copy).then_inc(ff_high, 1)

                    with act.Fori(0, tiles - 1) as i:
                        gu_pair(i)
                    gu_pair(tiles - 1)

                    def dn_pair(i, more=True):
                        for j in range(2):
                            if more:
                                split_high(layer, dn, i, j)
                            if c == 2:
                                n, t = sq_index[layer, "dn2"], i * 2 + j
                                act.wait_ge(slot_free[j], i + (USES[layer, dn] + 1))
                                if layer + 1 < DEPTH:
                                    for a, b, v in streams(True):
                                        last = f(hH[:, t, hcols(a, b)], x[:, t, a:b], ACT.Copy,
                                                 scale=gain[:, layer + 1, 0, bass.ds(t, 1), v])
                                    last.then_inc(high_ok, 1)
                                act.wait_ge(sq_used, i * 2 + (n + j - 1))
                                f(sq[j][:, 0:width], x[:, t, 0:width], ACT.Square).then_inc(sq_ok, 1)

                    if c == 2 and layer + 1 < DEPTH:
                        act.wait_ge(ada_cols, AG * (layer + 1) + 1)
                        act.wait_ge(gemm, 2 * USES[layer, "dn2"])
                        shift_high(layer + 1, 0)
                    if c < 2:
                        with act.Fori(0, PAIRS_OF[dn] - 1) as i:
                            dn_pair(i)
                    else:
                        for i in range(PAIRS_OF[dn] - 1):
                            dn_pair(i)
                    dn_pair(PAIRS_OF[dn] - 1, more=(layer, c) != (DEPTH - 1, 2))
                    ada_after(layer, dn)
            root((DEPTH, "n1"), NB)

        @block.vector
        def _(dve):
            chain = Chain(dve, dve_self)
            tt, stt, ts = nc.vector.tensor_tensor, nc.vector.scalar_tensor_tensor, nc.vector.tensor_scalar

            def f32(ap):
                return ap.bitcast(F32)

            def split_low(layer, name, i, j):
                dve.wait_ge(w_high, i * 2 + (2 * FIRST[layer, name] + j + 3))
                k = ktiles_after(layer, name, i)
                tt(wL[j][:, 0:k, :], raw[j][:, 0:k, :], f32(wH[j][:, 0:k, :]), ALU.subtract).then_inc(w_low, 1)

            def add_square(series, layer, k, width):
                n = sq_index[layer, series] + k
                dve.wait_ge(sq_ok, n + 1)
                if k:
                    dve.wait_ge(sq_used, n)
                    tt(ssum[:, 0:width], ssum[:, 0:width], sq[n % 2][:, 0:width], ALU.add).then_inc(sq_used, 1)
                else:
                    nc.vector.tensor_copy(ssum[:, 0:width], sq[n % 2][:, 0:width]).then_inc(sq_used, 1)

            def sum_done(series, layer, tiles):
                dve.wait_ge(sq_used, sq_index[layer, series] + tiles)
                nc.vector.tensor_copy(mx[:, 0:1], ssum[:, 0:1]).then_inc(sum_ok, 1)

            def diagonal(key, blocks):
                n = root_index[key] + 1
                dve.wait_ge(tok_root, n)
                chain.link(nc.vector.reciprocal(per_tok[:, 1, 0:blocks], per_tok[:, 0, 0:blocks]))
                for b in range(blocks):
                    last = ts(diag[:, b, :], ident[:], per_tok[:, 1, b:b + 1], None, ALU.mult)
                last.then_inc(diag_ok, 1)

            def low(n, k, src, scales):
                dve.wait_ge(high_ok, n + 1)
                for a, b, scale in scales:
                    last = stt(out=hL[:, k, hcols(a, b)], in0=src[:, a:b], scalar=scale,
                               in1=f32(hH[:, k, hcols(a, b)]), op0=ALU.mult, op1=ALU.subtract)
                last.then_inc(h_ok, 1)

            def shift_low(layer, shift):
                dve.wait_ge(sh_high, 2 * layer + (1 if shift == 0 else 2))
                for at in (N, HW - 2):
                    last = tt(hL[:, :, at:at + 2], mod[:, layer, shift * DT:(shift + 1) * DT, :],
                              f32(hH[:, :, at:at + 2]), ALU.subtract)
                last.then_inc(sh_ok, 1)

            def scale_product(slot, context):
                src, like = product(slot, context)
                nc.vector.tensor_copy(shifted[:, slot, :], shift_cols(slot))
                tt(like(tmp[slot]), src, like(rs), ALU.mult).then_inc(slot_free[slot], 1)

            def ada_columns(g):
                layer, gg = g // AG, g % AG
                dve.wait_ge(ada_tr, g + 1)
                for v in range(2):
                    src = bank[:, SMALL, :].rearrange("p (j q z) -> p q j z", q=4, z=32)[:, :, :, v]
                    dst = mod[:, layer, 16 * gg:16 * gg + 16, v].rearrange("p (q j) -> p q j", q=4)
                    o = layer * LAYER_COLS + OFF["b_ada"] + 16 * gg
                    last = tt(dst, src, par[:, o:o + 16].rearrange("p (q j) -> p q j", q=4), ALU.add)
                chain.link(last)
                if gg != 1:
                    which = gg // 2
                    vec = 1 if gg == 0 else 4
                    o = layer * LAYER_COLS + OFF["g_mix" if which == 0 else "g_ffn"]
                    for v in range(2):
                        last = stt(out=gain[:, layer, which, :, v], in0=mod[:, layer, vec * DT:(vec + 1) * DT, v],
                                   scalar=1.0, in1=par[:, o:o + DT], op0=ALU.add, op1=ALU.mult)
                    chain.link(last)
                nc.vector.tensor_copy(mx[:, 1:2], mod[:, layer, 16 * gg, 0:1]).then_inc(ada_cols, 1)

            def ada_after(layer, name):
                if (layer, name) in ADA_IN:
                    ada_columns(ADA_IN[layer, name])

            def update(layer, slot, use, gate, t, context):
                dve.wait_ge(slot_free[slot], use)
                for a, b, v in streams(context):
                    xt = x[:, t, a:b]
                    last = stt(out=xt, in0=bank[:, 2 * slot + (a >= N), 0:b - a],
                               scalar=mod[:, layer, bass.ds(t + gate * DT, 1), v], in1=xt, op0=ALU.mult, op1=ALU.add)
                last.then_inc(slot_free[slot], 1)

            def gate_out(layer, name, t, context):
                n = 2 * DT * layer + (DT if name == "ob" else 0) + t
                dve.wait_ge(gemm, 2 * USES[layer, name] + t + 1)
                if n >= 2:
                    dve.wait_ge(x_added, n - 1)
                for a, b, v in streams(context):
                    last = stt(out=tmp[t % 2][:, a:b], in0=bank[:, 2 * (t % 2) + (a >= N), 0:b - a],
                               scalar=mod[:, layer, 2 * DT + t, v:v + 1], in1=rs[:, a:b], op0=ALU.mult, op1=ALU.mult)
                last.then_inc(slot_free[t % 2], 1)

            def attention(layer):
                qs = queries(layer)
                order = [(q, i) for q in range(len(qs)) for i in range(GRP)]
                unit0 = GRP * group_index[layer, 0]

                def row_max(n):
                    u, (q, _) = unit0 + n, order[n]
                    w, c = P * len(qs[q][2]), u % 4
                    dve.wait_ge(s_ok, u + 1)
                    nc.vector.reduce_max(mx[:, c:c + 1], wide[:, 1024 * (u % 2):1024 * (u % 2) + w], AX.X)\
                        .then_inc(row_ok, 1)

                def neg_max(n):
                    u, (q, i) = unit0 + n, order[n]
                    c, h = u % 4, qs[q][0] * GRP + i
                    dve.wait_ge(row_ok, u + 1)
                    ts(nmax[:, c:c + 1], mx[:, c:c + 1], -SCALE, nsink[:, layer, h:h + 1], ALU.mult, ALU.min)\
                        .then_inc(max_ok, 1)

                def add_sink(n):
                    u, c = unit0 + n, (unit0 + n) % 4
                    dve.wait_ge(exp_ok, u + 1)
                    tt(psums[:, c:c + 1], psums[:, c:c + 1], esink[:, c:c + 1], ALU.add).then_inc(sink_ok, 1)

                def invert(n):
                    u, c = unit0 + n, (unit0 + n) % 4
                    dve.wait_ge(sink_ok, u + 1)
                    nc.vector.reciprocal(psums[:, c:c + 1], psums[:, c:c + 1]).then_inc(recip_ok, 1)

                def combine(h2):
                    n = 2 * h2 - unit0
                    (g, b, _), i = qs[order[n][0]], order[n][1]
                    dve.wait_ge(pv_low, h2 + 1)
                    for odd in range(2):
                        last = tt(aT[HD * odd:HD * odd + HD, (g * GRP + i) // 2, P * b:P * b + P],
                                  bank[0:HD, BC + h2 % 2, P * odd:P * odd + P],
                                  act_out[0:HD, P * (2 * (h2 % 2) + odd):P * (2 * (h2 % 2) + odd) + P], ALU.add)
                    last.then_inc(a_ok, 1)

                def prob_low(n):
                    u, (q, i) = unit0 + n, order[n]
                    w = len(qs[q][2])
                    dve.wait_ge(pt_high, u + 1)
                    tt(PT[:, 1, 0:w, i, :], wide[:, 512 * PTB:512 * PTB + P * w].rearrange("p (k q) -> p k q", k=w),
                       f32(PT[:, 0, 0:w, i, :]), ALU.subtract).then_inc(pt_ok, 1)

                row_max(0)
                neg_max(0)
                dve.wait_ge(v_high, layer + 1)
                tt(V2[:, :, :, 1, :], wide[:, 512 * PTB:512 * PTB + T].rearrange("p (t g d) -> p t g d", t=TB, g=KV),
                   f32(V2[:, :, :, 0, :]), ALU.subtract).then_inc(v_ready, 1)
                for n in range(-3, len(order)):
                    if 0 <= n + 2 < len(order):
                        add_sink(n + 2)
                        invert(n + 2)
                    if n >= 0:
                        prob_low(n)
                    if n + 4 < len(order):
                        row_max(n + 4)
                    if n + 4 < len(order):
                        neg_max(n + 4)
                    if n % 2 == 0 and n >= 4:
                        combine((unit0 + n) // 2 - 2)
                combine((unit0 + len(order)) // 2 - 2)
                combine((unit0 + len(order)) // 2 - 1)

            def rope(layer, t, j, context, split):
                turned = [(m + FREQS) % 32 for m in range(32)]
                r, rot = tmp[j], sq[0]
                dve.wait_ge(gemm, 2 * USES[layer, "qkv"] + t + 1)
                if layer + t:
                    dve.wait_ge(r_ok, 5 * layer + t)
                scale_product(j, split)
                split_low(layer, "qkv", t // 2, j)
                dve.wait_ge(slot_free[j], USES[layer, "qkv"] + t // 2 + 1)
                nc.vector.stream_shuffle(shifted_rot[:], shifted[:, j, :], turned)
                chain.link(nc.vector.stream_shuffle(rot[:, 0:N], r[:, 0:N], turned))
                if context:
                    ts(r[:, N:T], r[:, N:T], shifted[:, j, 1:2], None, ALU.add)
                stt(out=rot[:, 0:N], in0=rot[:, 0:N], scalar=shifted_rot[:, 0:1], in1=sinT[:], op0=ALU.add, op1=ALU.mult)
                chain.link(stt(out=r[:, 0:N], in0=r[:, 0:N], scalar=shifted[:, j, 0:1], in1=cosT[:], op0=ALU.add,
                               op1=ALU.mult))
                tt(r[:, 0:N], r[:, 0:N], rot[:, 0:N], ALU.add).then_inc(r_ok, 1)

            dve.wait_ge(par_in, 16)
            for layer in range(DEPTH):
                o = layer * LAYER_COLS + OFF["sink"]
                ts(nsink[:, layer, :], par[:, o:o + HEADS], -1.0, None, ALU.mult).then_inc(nsink_ok, 1)
            for k in range(DT):
                add_square("x", 0, k, T)
            sum_done("x", 0, DT)
            dve.wait_ge(const_in, 48)
            dve.wait_ge(nsink_ok, DEPTH)
            diagonal((0, "n1"), TB)
            for j in range(2):
                dve.wait_ge(w_high, j + 1)
                tt(wL[j][:], raw[j][:], f32(wH[j][:]), ALU.subtract).then_inc(w_low, 1)
            ada_columns(0)
            shift_low(0, 0)
            for k in range(DT):
                low(k, k, x[:, k, :], gains(0, 0, True, k))
            for layer in range(DEPTH):
                context = layer == 0
                width, blocks = (T, TB) if context else (N, NB)
                if layer:
                    diagonal((layer, "n1"), TB)
                dve.wait_ge(rs_ok, rs_index[layer, "n1"] + 1)

                def u_pair(i):
                    use = USES[layer, "u"] + i
                    dve.wait_ge(gemm, 2 * use + 1)
                    scale_product(0, context)
                    split_low(layer, "u", i, 0)
                    convolve(CONV_IN_U[layer][i][0])
                    dve.wait_ge(gemm, 2 * use + 2)
                    scale_product(1, context)
                    split_low(layer, "u", i, 1)
                    dve.wait_ge(slot_free[0], use + 1)
                    dve.wait_ge(gate_ok, i + gates_before(layer, "u") + 1)
                    for a, b, v in streams(context):
                        at = PAD if a == 0 else CC + PAD
                        last = stt(out=z[:, i, at:at + b - a], in0=tmp[0][:, a:b], scalar=shifted[:, 0, v:v + 1],
                                   in1=act_out[:, a:b], op0=ALU.add, op1=ALU.mult)
                    last.then_inc(z_ok, 1)
                    dve.wait_ge(z_ok, CT * layer + i + 1)

                cw = CVW if layer == 0 else N
                taps = list(DVE_TAPS)

                def convolve(n):
                    for _ in range(min(n, len(taps))):
                        k, tap = taps.pop(0)
                        acc, src, w = cv[:, k, 0:cw], z[:, k, tap:tap + cw], col("w_dw", tap * CT + k, layer)
                        if k in POOL_TILES:
                            acc = ssum[:, 0:cw]
                            if tap == 0:
                                dve.wait_ge(zpad, layer + 1)
                                chain.link(ts(acc, src, w, None, ALU.mult))
                            elif tap < SHARED - 1:
                                chain.link(stt(out=acc, in0=src, scalar=w, in1=acc, op0=ALU.mult, op1=ALU.add))
                            else:
                                stt(out=acc, in0=src, scalar=w, in1=acc, op0=ALU.mult, op1=ALU.add).then_inc(shared_ok, 1)
                        elif tap == 0:
                            dve.wait_ge(zpad, layer + 1)
                            chain.link(ts(acc, src, w, col("b_dw", k, layer), ALU.mult, ALU.add))
                        else:
                            chain.link(stt(out=acc, in0=src, scalar=w, in1=acc, op0=ALU.mult, op1=ALU.add))

                for i in range(PAIRS_OF["u"]):
                    u_pair(i)
                    if layer and i == 0:
                        ada_columns(ADA_IN[0, "dn2"])
                    convolve(CONV_IN_U[layer][i][1])

                for i in range(3):
                    for j in range(2):
                        t = 2 * i + j
                        if 0 < t < 5:
                            rope(layer, t, j, context, context)
                            convolve(CONV_IN_QKV[layer][t])
                            dve.wait_ge(qk_high, 5 * layer + t + 1)
                            tt(Q2[HD:P, 2 * t - 2, 0:width], tmp[j][0:HD, 0:width], f32(Q2[0:HD, 2 * t - 2, 0:width]),
                               ALU.subtract)
                            tt(Q2[0:HD, 2 * t - 1, 0:width], tmp[j][HD:P, 0:width], f32(Q2[HD:P, 2 * t - 1, 0:width]),
                               ALU.subtract).then_inc(qk_ok, 1)
                        elif t == 0:
                            rope(layer, t, j, True, True)
                            convolve(CONV_IN_QKV[layer][t])
                            dve.wait_ge(qk_high, 5 * layer + t + 1)
                            for g in range(KV):
                                for half in range(2):
                                    last = tt(K2[HD * half:HD * half + HD, g, 1, :], tmp[0][HD * g:HD * g + HD, :],
                                              f32(K2[HD * g:HD * g + HD, g, 0, :]), ALU.subtract)
                            last.then_inc(qk_ok, 1)
                        else:
                            dve.wait_ge(gemm, 2 * USES[layer, "qkv"] + t + 1)
                            dve.wait_ge(qk_ok, 5 * layer + 4)
                            scale_product(1, True)
                            split_low(layer, "qkv", i, j)
                            convolve(CONV_IN_QKV[layer][t])
                        if t == 1:
                            ada_after(layer, "u")
                ada_after(layer, "qkv")
                attention(layer)

                n = h_index[layer, "an"]
                dve.wait_ge(conv_ok, len(POOL_TILES) * layer + 1)
                for k in range(CT):
                    low(n + k, k, aT[:, k, :], [(a, b, col("g_attn", k, layer)) for a, b, _ in streams(context)])
                for k in range(CT):
                    add_square("an", layer, k, width)
                sum_done("an", layer, CT)
                dve.wait_ge(conv_ok, len(POOL_TILES) * (layer + 1))
                diagonal((layer, "an"), blocks)

                chain.link(tt(ssum[:, 0:cw], cv[:, 0, 0:cw], cv[:, 1, 0:cw], ALU.add))
                chain.link(tt(ssum[:, 0:cw], ssum[:, 0:cw], cv[:, 2, 0:cw], ALU.add))
                tt(ssum[:, 0:cw], ssum[:, 0:cw], cv[:, 3, 0:cw], ALU.add).then_inc(sum_ok, 1)
                dve.wait_ge(rs_ok, rs_index[layer, "an"] + 1)
                for t in range(DT - 2):
                    if t == 4:
                        diagonal((layer, "var"), blocks)
                    gate_out(layer, "oa", t, context)
                    if t % 2:
                        split_low(layer, "oa", t // 4, t // 2 % 2)
                    if t == 1:
                        dve.wait_ge(bc_ok, stat_index[layer, "mean"] + 1)
                        for k in range(CT):
                            for a, b, _v in streams(context):
                                at = a if a == 0 else CC
                                last = stt(out=z[:, k, a:b], in0=wide[:, 512 * BC + a:512 * BC + b], scalar=-1.0 / CW,
                                           in1=cv[:, k, at:at + b - a], op0=ALU.mult, op1=ALU.add)
                            last.then_inc(ln_d, 1)
                        for k in range(CT):
                            add_square("var", layer, k, width)
                        sum_done("var", layer, CT)
                    if t == 4:
                        dve.wait_ge(bc_ok, stat_index[layer, "var"] + 1)
                        for k in range(CT):
                            dve.wait_ge(sq_ok, sq_index[layer, "var"] + k + 1)
                            zk = z[:, k, 0:width]
                            stt(out=zk, in0=zk, scalar=col("ln_g", k, layer), in1=wide[:, 512 * BC:512 * BC + width],
                                op0=ALU.mult, op1=ALU.mult).then_inc(ln_y, 1)
                n = h_index[layer, "cn"]
                for k in range(CT):
                    low(n + k, CT + k, cv[:, k, :], [(a, b, col("g_conv", k, layer)) for a, b, _ in streams(context)])
                    add_square("cn", layer, k, width)
                    if k in (1, 2):
                        gate_out(layer, "oa", DT - 3 + k, context)
                sum_done("cn", layer, CT)
                split_low(layer, "oa", 1, 1)
                diagonal((layer, "cn"), blocks)
                shift_low(layer, 3)

                dve.wait_ge(rs_ok, rs_index[layer, "cn"] + 1)
                n = h_index[layer, "n2"]
                for t in range(DT):
                    gate_out(layer, "ob", t, context)
                    if t % 2:
                        split_low(layer, "ob", t // 4, t // 2 % 2)
                    if t:
                        add_square("ob", layer, t - 1, width)
                        if t <= CT:
                            low(n + t - 1, t - 1, x[:, t - 1, :], gains(layer, 1, context, t - 1))
                for t in range(CT, DT):
                    low(n + t, t, x[:, t, :], gains(layer, 1, context, t))
                add_square("ob", layer, DT - 1, width)
                sum_done("ob", layer, DT)
                diagonal((layer, "n2"), blocks)
                dve.wait_ge(rs_ok, rs_index[layer, "n2"] + 1)

                for c, tiles in enumerate(CHUNKS):
                    gu, dn = f"gu{c}", f"dn{c}"
                    ff = layer * FT + sum(CHUNKS[:c])

                    def gu_pair(i):
                        dve.wait_ge(gemm, i * 2 + (2 * USES[layer, gu] + 1))
                        scale_product(0, context)
                        split_low(layer, gu, i, 0)
                        dve.wait_ge(gemm, i * 2 + (2 * USES[layer, gu] + 2))
                        scale_product(1, context)
                        split_low(layer, gu, i, 1)
                        dve.wait_ge(slot_free[1], i + (USES[layer, gu] + 1))
                        dve.wait_ge(gate_ok, i + (gates_before(layer, "gu") + sum(CHUNKS[:c]) + 1))
                        for a, b, v in streams(context):
                            last = stt(out=tmp[1][:, a:b], in0=tmp[1][:, a:b], scalar=shifted[:, 1, v:v + 1],
                                       in1=act_out[:, a:b], op0=ALU.add, op1=ALU.mult)
                        last.then_inc(ff_ok, 1)
                        dve.wait_ge(ff_high, i + (ff + 1))
                        tt(aL[:, i, 0:width], tmp[1][:, 0:width], f32(aH[:, i, 0:width]), ALU.subtract).then_inc(ff_low, 1)
                        dve.wait_ge(ff_low, i + (ff + 1))

                    with dve.Fori(0, tiles - 1) as i:
                        gu_pair(i)
                    gu_pair(tiles - 1)

                    def dn_pair(i, more=True):
                        for j in range(2):
                            t = i * 2 + j
                            if more:
                                split_low(layer, dn, i, j)
                            dve.wait_ge(gemm, i * 2 + (2 * USES[layer, dn] + j + 1))
                            update(layer, j, i + USES[layer, dn], 5, t, context)
                            if c == 2:
                                if layer + 1 < DEPTH:
                                    dve.wait_ge(high_ok, t + (h_index[layer + 1, "n1"] + 1))
                                    for a, b, v in streams(True):
                                        last = stt(out=hL[:, t, hcols(a, b)], in0=x[:, t, a:b],
                                                   scalar=gain[:, layer + 1, 0, bass.ds(t, 1), v],
                                                   in1=f32(hH[:, t, hcols(a, b)]), op0=ALU.mult, op1=ALU.subtract)
                                    last.then_inc(h_ok, 1)
                                n = sq_index[layer, "dn2"]
                                dve.wait_ge(sq_ok, i * 2 + (n + j + 1))
                                dve.wait_ge(sq_used, i * 2 + (n + j))
                                tt(ssum[:, 0:width], ssum[:, 0:width], sq[j][:, 0:width], ALU.add).then_inc(sq_used, 1)

                    if c == 2:
                        if layer + 1 < DEPTH:
                            shift_low(layer + 1, 0)
                        chain.link(nc.vector.memset(ssum[:, 0:width], 0.0))
                    with dve.Fori(0, PAIRS_OF[dn] - 1) as i:
                        dn_pair(i)
                    dn_pair(PAIRS_OF[dn] - 1, more=(layer, c) != (DEPTH - 1, 2))
                    if c == 2:
                        sum_done("dn2", layer, DT)
                    if c < 2:
                        ada_after(layer, dn)
            diagonal((DEPTH, "n1"), NB)
            dve.wait_ge(bc_ok, stat_index[DEPTH, "n1"] + 1)
            for k in range(DT):
                stt(out=x[:, k, 0:N], in0=x[:, k, 0:N], scalar=col("g_final", k), in1=wide[:, 512 * BC:512 * BC + N],
                    op0=ALU.mult, op1=ALU.mult).then_inc(y_ok, 1)

        @block.gpsimd
        def _(pool):
            chain = Chain(pool, pool_self)
            nc.gpsimd.memset(cond[:], 0.0).then_inc(consts, 1)
            nc.gpsimd.memset(eps[:], EPS).then_inc(consts, 1)
            nc.gpsimd.memset(ones[:], 1.0).then_inc(consts, 1)
            nc.gpsimd.memset(mean_col[:, 0:1], 1.0 / D)
            nc.gpsimd.memset(mean_col[:, 1:2], 1.0 / CW).then_inc(consts, 1)
            pool.wait_ge(par_in, 16)
            for layer in range(DEPTH):
                if layer:
                    pool.wait_ge(gemm, 2 * USES[layer, "u"])
                pads = [(0, PAD), (PAD + N, PAD + N + 2 * PAD), (ZW - PAD, ZW)][:3 if layer == 0 else 2]
                for a, b in pads:
                    last = nc.gpsimd.memset(z[:, :, a:b], 0.0)
                last.then_inc(zpad, 1)
                pool.wait_ge(zpad, layer + 1)
                cw = CVW if layer == 0 else N
                for k in POOL_TILES:
                    pool.wait_ge(z_ok, CT * layer + k + 1)
                    acc = cv[:, k, 0:cw]
                    first = SHARED if k == 0 else 0
                    chain.link(nc.gpsimd.tensor_scalar(acc, z[:, k, first:first + cw], col("w_dw", first * CT + k, layer),
                                                       col("b_dw", k, layer), ALU.mult, ALU.add))
                    for tap in range(first + 1, TAPS):
                        chain.link(nc.gpsimd.tensor_scalar(scratch[:, 0:cw], z[:, k, tap:tap + cw],
                                                           col("w_dw", tap * CT + k, layer), 0.0, ALU.mult, ALU.add))
                        last = nc.gpsimd.tensor_tensor(acc, acc, scratch[:, 0:cw], ALU.add)
                        if tap < TAPS - 1 or k == 0:
                            chain.link(last)
                    if k == 0:
                        pool.wait_ge(shared_ok, layer + 1)
                        last = nc.gpsimd.tensor_tensor(acc, acc, ssum[:, 0:cw], ALU.add)
                    last.then_inc(conv_ok, 1)
                for n in range(2 * DT):
                    name, t = ("oa", "ob")[n // DT], n % DT
                    pool.wait_ge(slot_free[t % 2], USES[layer, name] + t // 2 + 1)
                    w = T if layer == 0 else N
                    if n >= DT:
                        pool.wait_ge(x_added, 2 * DT * layer + n - DT + 1)
                    nc.gpsimd.tensor_tensor(x[:, t, 0:w], x[:, t, 0:w], tmp[t % 2][:, 0:w], ALU.add).then_inc(x_added, 1)


def ktiles_after(layer, name, i):
    p = FIRST[layer, name] + (i if isinstance(i, int) else 0) + 1
    return KTILES[min(p, PAIRS - 1)] if isinstance(i, int) else KTILES[FIRST[layer, name]]


def weight_blocks(w, outs, k_tiles):
    blocks = np.stack([np.concatenate([w[:, P * k:P * k + P, o:o + P] for k in ks], axis=2)
                       for o, ks in zip(outs, k_tiles)], axis=1)
    layers, n = blocks.shape[:2]
    return np.ascontiguousarray(blocks.reshape(layers, n // 2, 2, P, -1).transpose(0, 2, 1, 3, 4))


def host_constants():
    tok = np.arange(N)
    freqs = (np.float32(10000.0) ** (-np.arange(FREQS, dtype=np.float32) / np.float32(FREQS))).astype(np.float32)
    ang = np.zeros((HD, N), np.float32)
    for d in range(HD):
        pos = (tok // GRID_W if d < HD // 2 else tok % GRID_W).astype(np.float32)
        ang[d] = pos * freqs[d % FREQS]
    ang = np.concatenate([ang, ang]).astype(np.float64)
    sign = np.where(np.arange(P) % (2 * FREQS) < FREQS, -1.0, 1.0)[:, None]
    rope = np.stack([np.cos(ang), sign * np.sin(ang)]).astype(np.float32)
    q, k = np.arange(P)[:, None], np.arange(P)[None, :]
    masks = np.concatenate([np.where(k >= q, 0.0, MASKED), np.where(k <= q, 0.0, MASKED)], axis=1).astype(np.float32)
    return rope, np.eye(P, dtype=np.float32), masks


def kernel(**inputs):
    import concourse.bacc as bacc
    from concourse.bass_utils import run_bass_kernel_spmd

    a = {k: np.asarray(v) for k, v in inputs.items()}

    def cols(v):
        return v.reshape(-1, P).T

    table = []
    for l in range(DEPTH):
        table += [cols(a[n][l]) for n in ("b_ada", "g_mix", "g_ffn", "g_attn_out", "g_conv_out", "b_dw", "ln_g", "ln_b", "w_dw")]
        table.append(np.broadcast_to(a["attn_sink"][l][None, :], (P, HEADS)))
    table.append(cols(a["g_final"]))
    table.append(np.stack([cols(a["c"][0]), cols(a["c_ctx"])], axis=2).reshape(P, 2 * DT))
    tokens = np.concatenate([a["x"][0], a["ctx"][0]], axis=0)

    q_k_v, half = AW + 2 * KV * HD, AW + 2 * KV * HD + CW
    mix = [o for i in range(CT) for o in (q_k_v + P * i, half + P * i)] + [P * i for i in (CT, *range(CT), CT + 1)]
    w_mix = weight_blocks(a["w_in"], mix, [range(DT)] * len(mix))
    wo = a["w_out"].reshape(DEPTH, 2, CT, P, DT // 2, 2, P)
    wo = wo.transpose(0, 1, 4, 3, 5, 2, 6).reshape(DEPTH, 2, 2, 2, P, 2 * CT * P)
    w_out = np.ascontiguousarray(wo.transpose(0, 3, 1, 2, 4, 5).reshape(DEPTH, 2, 4, P, 2 * CT * P))
    gu = [o for i in range(FT) for o in (P * i, D_FF + P * i)]
    w_gu = weight_blocks(a["w_gate_up"], gu, [range(DT)] * len(gu))
    dn = [weight_blocks(a["w_down"], [P * i for i in range(DT)],
                        [range(sum(CHUNKS[:c]), sum(CHUNKS[:c + 1]))] * DT) for c in range(3)]
    w_ada = np.ascontiguousarray(a["w_ada"].reshape(DEPTH, DT, P, AG, AGW).transpose(0, 3, 1, 2, 4)
                                 .reshape(DEPTH * AG, DT, P, AGW))
    rope, ident, masks = host_constants()
    arrays = {
        "xT": np.ascontiguousarray(tokens.T.reshape(DT, P, T)), "params": np.ascontiguousarray(np.concatenate(table, axis=1)),
        "w_ada": w_ada, "w_mix": w_mix, "w_out": w_out, "w_gu": w_gu, "w_dn0": dn[0], "w_dn1": dn[1], "w_dn2": dn[2],
        "rope": rope, "ident_in": ident, "masks_in": masks,
    }
    nc = bacc.Bacc("TRN2", target_bir_lowering=False, num_devices=1)
    args = {n: nc.dram_tensor(f"in_{n}", v.shape, mybir.dt.from_np(v.dtype), kind="ExternalInput").ap()
            for n, v in arrays.items()}
    out = nc.dram_tensor("out_yT", (DT, P, N), F32, kind="ExternalOutput").ap()
    hybrid_backbone(nc, *args.values(), out)
    r = run_bass_kernel_spmd(nc, [{f"in_{n}": v for n, v in arrays.items()}], core_ids=[0])
    y = r.results[0]["out_yT"]
    return np.ascontiguousarray(y.reshape(D, N).T).reshape(1, N, D)
```
